# Optimizing a Trainium2 kernel written in Bass

```python
import jax, jax.numpy as jnp
from jax import lax
import numpy as np

D_MODEL = 1024
BATCH = 1
SEQ = 1024
DEPTH = 1

D_MIX = D_MODEL
CONV_WIDTH = D_MIX // 2
CONV_K = 3
RWKV_WIDTH = D_MIX - CONV_WIDTH
RWKV_HEAD = 64
RWKV_HEADS = RWKV_WIDTH // RWKV_HEAD
LORA_DECAY = 64
LORA_ICLR = 64
LORA_GATE = 128
RWKV_COLS = 3 * RWKV_WIDTH + LORA_DECAY + LORA_ICLR + LORA_GATE
IN_COLS = 3 * CONV_WIDTH + RWKV_COLS
N_EXPERTS = 32
TOP_K = 4
D_FF = D_MODEL
SWIGLU_LIMIT = 7.0
SWIGLU_ALPHA = 1.702
EXPERT_BLOCK = 128
RMS_EPS = 1e-5
GN_EPS = 64e-5

kernel_name = "hybrid_shortconv_rwkv7_moe_block"

def rms_norm(x, w):
    xf = x.astype(jnp.float32)
    y = xf * lax.rsqrt(jnp.mean(xf * xf, axis=-1, keepdims=True) + RMS_EPS)
    return (y * w.astype(jnp.float32)).astype(x.dtype)

def token_shift(p, mu):
    prev = jnp.pad(p, ((0, 0), (1, 0), (0, 0)))[:, :-1]
    return p + (prev - p) * mu

def causal_dwconv(u, w):
    S = u.shape[1]
    up = jnp.pad(u, ((0, 0), (CONV_K - 1, 0), (0, 0)))
    y = w[0] * up[:, 0:S]
    for j in range(1, CONV_K):
        y = y + w[j] * up[:, j:j + S]
    return y

def rwkv7_scan(r, w, k, v, a, b):
    Bsz, S, H, N = r.shape

    def step(state, inp):
        r_t, w_t, k_t, v_t, a_t, b_t = inp
        sa = jnp.einsum('bhij,bhj->bhi', state, a_t)
        state = (state * w_t[:, :, None, :]
                 + sa[..., :, None] * b_t[..., None, :]
                 + v_t[..., :, None] * k_t[..., None, :])
        y_t = jnp.einsum('bhij,bhj->bhi', state, r_t)
        return state, y_t

    xs = (jnp.moveaxis(r, 1, 0), jnp.moveaxis(w, 1, 0), jnp.moveaxis(k, 1, 0),
          jnp.moveaxis(v, 1, 0), jnp.moveaxis(a, 1, 0), jnp.moveaxis(b, 1, 0))
    s0 = jnp.zeros((Bsz, H, N, N), jnp.float32)
    _, ys = lax.scan(step, s0, xs)
    return jnp.moveaxis(ys, 0, 1)

def hybrid_mixer(xn, w_in, conv_w, mu_shift, w0, w_decay_up, a0, w_iclr_up, w_gate_up,
                 k_k, k_a, r_k, ln_x_w, ln_x_b, w_out):
    f32 = jnp.float32
    Bsz, S, _ = xn.shape
    H, N = RWKV_HEADS, RWKV_HEAD
    p = xn @ w_in
    c_b, c_c, c_h, p_rwkv = jnp.split(p, [CONV_WIDTH, 2 * CONV_WIDTH, 3 * CONV_WIDTH], axis=-1)

    y_conv = c_b * causal_dwconv(c_c * c_h, conv_w)

    q = token_shift(p_rwkv, mu_shift)
    o1 = 3 * RWKV_WIDTH
    r, k, v, d_w, d_a, d_g = jnp.split(
        q, [RWKV_WIDTH, 2 * RWKV_WIDTH, o1, o1 + LORA_DECAY, o1 + LORA_DECAY + LORA_ICLR], axis=-1)
    w_log = -jax.nn.softplus(-(w0 + jnp.tanh(d_w) @ w_decay_up).astype(f32)) - 0.5
    decay = jnp.exp(-jnp.exp(w_log))
    iclr = jax.nn.sigmoid((a0 + d_a @ w_iclr_up).astype(f32))
    g = jax.nn.sigmoid(d_g) @ w_gate_up

    def heads(t):
        return t.astype(f32).reshape(Bsz, S, H, N)

    r, k, v, decay, iclr = heads(r), heads(k), heads(v), heads(decay), heads(iclr)
    kk = k * k_k.astype(f32).reshape(H, N)
    kk = kk / jnp.maximum(jnp.linalg.norm(kk, axis=-1, keepdims=True), 1e-12)
    k = k * (1.0 + (iclr - 1.0) * k_a.astype(f32).reshape(H, N))
    y = rwkv7_scan(r, decay, k, v, -kk, kk * iclr)
    mean = jnp.mean(y, axis=-1, keepdims=True)
    var = jnp.mean(jnp.square(y - mean), axis=-1, keepdims=True)
    y = ((y - mean) * lax.rsqrt(var + GN_EPS) * ln_x_w.astype(f32).reshape(H, N)
         + ln_x_b.astype(f32).reshape(H, N))
    y = y + jnp.sum(r * k * r_k.astype(f32), axis=-1, keepdims=True) * v
    y_rwkv = y.reshape(Bsz, S, RWKV_WIDTH).astype(xn.dtype) * g

    return jnp.concatenate([y_conv, y_rwkv], axis=-1) @ w_out

def moe_ffn(xn, router_w, router_b, gu_w, gu_b, dn_w, dn_b):
    f32 = jnp.float32
    Bsz, S, D = xn.shape
    T = Bsz * S
    xt = xn.reshape(T, D)
    logits = xt.astype(f32) @ router_w.astype(f32) + router_b.astype(f32)
    top_vals, top_idx = lax.top_k(logits, TOP_K)
    gates = jax.nn.softmax(top_vals, axis=-1)

    n_pairs = T * TOP_K
    flat_e = top_idx.reshape(-1).astype(jnp.int32)
    flat_tok = jnp.arange(n_pairs, dtype=jnp.int32) // TOP_K
    flat_g = gates.reshape(-1)
    order = jnp.argsort(flat_e)
    se = flat_e[order]
    counts = jnp.bincount(flat_e, length=N_EXPERTS)
    starts = jnp.cumsum(counts) - counts
    pcounts = (counts + EXPERT_BLOCK - 1) // EXPERT_BLOCK * EXPERT_BLOCK
    pends = jnp.cumsum(pcounts)
    pstarts = pends - pcounts
    dest = pstarts[se] + (jnp.arange(n_pairs, dtype=jnp.int32) - starts[se])
    n_rows = -(-n_pairs // EXPERT_BLOCK) * EXPERT_BLOCK + N_EXPERTS * EXPERT_BLOCK
    n_blocks = n_rows // EXPERT_BLOCK
    row_tok = jnp.zeros((n_rows,), jnp.int32).at[dest].set(flat_tok[order])
    row_gate = jnp.zeros((n_rows,), f32).at[dest].set(flat_g[order])
    blk_e = jnp.minimum(
        jnp.searchsorted(pends, jnp.arange(n_blocks, dtype=jnp.int32) * EXPERT_BLOCK, side='right'),
        N_EXPERTS - 1).astype(jnp.int32)
    xs = xt[row_tok].reshape(n_blocks, EXPERT_BLOCK, D)

    def expert_block(args):
        xb, e = args
        h = xb @ gu_w[e] + gu_b[e]
        x_glu = jnp.minimum(h[:, 0::2], SWIGLU_LIMIT)
        x_lin = jnp.clip(h[:, 1::2], -SWIGLU_LIMIT, SWIGLU_LIMIT)
        act = x_glu * jax.nn.sigmoid(SWIGLU_ALPHA * x_glu) * (x_lin + 1.0)
        return act @ dn_w[e] + dn_b[e]

    yb = lax.map(expert_block, (xs, blk_e)).reshape(n_rows, D)
    contrib = (yb.astype(f32) * row_gate[:, None]).astype(xt.dtype)
    y = jnp.zeros((T, D), xt.dtype).at[row_tok].add(contrib)
    return y.reshape(Bsz, S, D)

def setup_inputs(seed: int = 0) -> dict:
    key = jax.random.key(seed)
    ks = jax.random.split(key, 26)
    f32 = jnp.float32
    L, D, H, N = DEPTH, D_MODEL, RWKV_HEADS, RWKV_HEAD

    def nrm(k, shape, scale):
        return jax.random.normal(k, shape, f32) * scale

    return {
        "x": nrm(ks[0], (BATCH, SEQ, D), 1.0),
        "norm_mix_w": 1.0 + nrm(ks[1], (L, D), 0.02),
        "w_in": nrm(ks[2], (L, D, IN_COLS), D ** -0.5),
        "conv_w": nrm(ks[3], (L, CONV_K, CONV_WIDTH), CONV_K ** -0.5),
        "mu_shift": jax.random.uniform(ks[4], (L, RWKV_COLS), f32, 0.0, 1.0),
        "w0": jax.random.uniform(ks[5], (L, RWKV_WIDTH), f32, -6.0, 1.0),
        "w_decay_up": nrm(ks[6], (L, LORA_DECAY, RWKV_WIDTH), 0.1),
        "a0": nrm(ks[7], (L, RWKV_WIDTH), 0.3),
        "w_iclr_up": nrm(ks[8], (L, LORA_ICLR, RWKV_WIDTH), 0.1),
        "w_gate_up": nrm(ks[9], (L, LORA_GATE, RWKV_WIDTH), LORA_GATE ** -0.5),
        "k_k": 0.85 + nrm(ks[10], (L, RWKV_WIDTH), 0.05),
        "k_a": 1.0 + nrm(ks[11], (L, RWKV_WIDTH), 0.05),
        "r_k": nrm(ks[12], (L, H, N), 0.1),
        "ln_x_w": 1.0 + nrm(ks[13], (L, RWKV_WIDTH), 0.02),
        "ln_x_b": nrm(ks[14], (L, RWKV_WIDTH), 0.02),
        "w_out": nrm(ks[15], (L, D_MIX, D), D_MIX ** -0.5),
        "norm_ffn_w": 1.0 + nrm(ks[16], (L, D), 0.02),
        "router_w": nrm(ks[17], (L, D, N_EXPERTS), D ** -0.5),
        "router_b": nrm(ks[18], (L, N_EXPERTS), 0.01),
        "gu_w": nrm(ks[19], (L, N_EXPERTS, D, 2 * D_FF), D ** -0.5),
        "gu_b": nrm(ks[20], (L, N_EXPERTS, 2 * D_FF), 0.01),
        "dn_w": nrm(ks[21], (L, N_EXPERTS, D_FF, D), D_FF ** -0.5),
        "dn_b": nrm(ks[22], (L, N_EXPERTS, D), 0.01),
        "norm_final_w": 1.0 + nrm(ks[23], (D,), 0.02),
    }

def reference(x, norm_mix_w, w_in, conv_w, mu_shift, w0, w_decay_up, a0, w_iclr_up, w_gate_up,
              k_k, k_a, r_k, ln_x_w, ln_x_b, w_out, norm_ffn_w, router_w, router_b,
              gu_w, gu_b, dn_w, dn_b, norm_final_w):
    h = x
    for l in range(DEPTH):
        h = h + hybrid_mixer(rms_norm(h, norm_mix_w[l]), w_in[l], conv_w[l], mu_shift[l], w0[l],
                             w_decay_up[l], a0[l], w_iclr_up[l], w_gate_up[l], k_k[l], k_a[l],
                             r_k[l], ln_x_w[l], ln_x_b[l], w_out[l])
        h = h + moe_ffn(rms_norm(h, norm_ffn_w[l]), router_w[l], router_b[l],
                        gu_w[l], gu_b[l], dn_w[l], dn_b[l])
    return rms_norm(h, norm_final_w)


_drawn_inputs = setup_inputs


def setup_inputs(seed=0):
    import zlib

    import numpy as np

    out = dict(_drawn_inputs(seed))
    spreads = {}
    factors = {'ln_x_b': 3.048, 'gu_b': 8.0, 'dn_b': 8.0, 'norm_final_w': 2.907}
    for name, (base, spread) in spreads.items():
        noise = np.random.default_rng([zlib.crc32(name.encode()), seed]).standard_normal(out[name].shape)
        drawn = base * np.exp(spread * noise) if base else spread * noise
        out[name] = __import__('jax').numpy.asarray(drawn.astype(out[name].dtype))
    for name, factor in factors.items():
        out[name] = (out[name] * factor).astype(out[name].dtype)
    return out
```

```python
import concourse.bass as bass
from concourse import mybir
from contextlib import ExitStack
import math
import numpy as np

FP = mybir.dt.float32
I32 = mybir.dt.int32
ALU = mybir.AluOpType
ACT = mybir.ActivationFunctionType
AX = mybir.AxisListType

P = 128
T = 1024
D = 1024
KT = D // P
TT = T // P
HALF = 512
CONV = 512
RW = 512
RT = RW // P
N = 64
L = 64
NCH = T // L
LORA = 64
E = 32
TOPK = 4
F = 1024
C = 160
C2 = C - P
ROUNDS = -(-T // C)
LIST = ROUNDS * C
PAIRS = T * TOPK
SKIP = 1 << 20
RMS_EPS = 1e-5
GN_EPS = 64e-5
KAPPA = math.exp(-0.5)
LIMIT = 7.0
ALPHA = 1.702
LEVELS = [2, 4, 8, 16, 32]

MU, W0, A0, KKW, KAW, RKW, LNW, LNB, CVW = 0, 14, 18, 22, 26, 30, 34, 38, 42
NPRM = 54

K_ID, K_ONES2, K_MG, K_ID2, K_M1, K_ME, K_BD, K_MTB = 0, 128, 256, 384, 448, 512, 832, 960
K_MIX = 960 + 128 * 6
K_TRI, K_ALL, K_EXP, K_TOK = K_MIX, K_MIX + 128, K_MIX + 256, K_MIX + 288
NCONST = K_MIX + 288 + TT


def constants():
    c = np.zeros((P, NCONST), np.float32)
    p = np.arange(P)[:, None]
    q = np.arange(P)[None, :]
    t = np.arange(L)[None, :]
    pl = p % L
    c[:, K_ID:K_ID + P] = p == q
    c[:, K_ONES2:K_ONES2 + P] = p // N == q // N
    c[:, K_MG:K_MG + L] = pl < t
    c[:, K_MG + L:K_MG + 2 * L] = pl <= t
    c[:, K_ID2:K_ID2 + L] = pl == t
    same = p // L == q // L

    def off(b, row, col):
        return (row // b % 2 == 1) & (col // b == row // b - 1)

    c[:, K_M1:K_M1 + L] = off(1, pl, t)
    for n, b in enumerate(LEVELS):
        c[:, K_ME + n * L:K_ME + (n + 1) * L] = off(b, pl, t)
        c[:, K_MTB + n * P:K_MTB + (n + 1) * P] = same & off(b, pl, q % L)
    c[:, K_BD:K_BD + P] = same & off(1, q % L, pl)
    c[:, K_MTB + 5 * P:K_MTB + 6 * P] = same
    c[:, K_TRI:K_TRI + P] = p < q
    c[:, K_ALL:K_ALL + P] = 1.0
    c[:, K_EXP:K_EXP + E] = np.arange(E)[None, :]
    c[:, K_TOK:K_TOK + TT] = np.arange(TT)[None, :] * P + p
    return c


class Chain:

    def __init__(self, eng, sem, base=0):
        self.eng, self.sem, self.base, self.n = eng, sem, base, 0

    def link(self, ins):
        self.n += 1
        ins.then_inc(self.sem, 1)
        self.eng.wait_ge(self.sem, self.base + self.n)


def build(nc, x, w_in_t, prm_d, lora_d, wgate_d, normw_d, w_out, router_w, router_b, gub_d, gu_w, dn_w,
          dn_b, consts_d, list0_d, out, conv_d, bonus_d, xn_d, pair_d, list_d, flag_d, stop=99):
    ctx = ExitStack()
    with ctx:
        def sem(name):
            return ctx.enter_context(nc.semaphore(name))

        def sb(name, shape, dt=FP):
            return ctx.enter_context(nc.sbuf_tensor(name, shape, dt))

        arena = sb("arena", [P, 196 * 256])

        def at(kb, *shape):
            n = math.prod(shape)
            o = int(kb * 256)
            v = arena[:, o:o + n]
            if len(shape) == 2:
                v = v.rearrange("p (a b) -> p a b", b=shape[1])
            elif len(shape) == 3:
                v = v.rearrange("p (a b c) -> p a b c", b=shape[1], c=shape[2])
            elif len(shape) == 4:
                v = v.rearrange("p (a b c d) -> p a b c d", b=shape[1], c=shape[2], d=shape[3])
            return v

        ps = ctx.enter_context(nc.psum_tensor("ps", [P, 8, HALF], FP))
        cst = sb("cst", [P, K_MIX])
        prm = sb("prm_sb", [P, NPRM])
        omka = sb("omka", [P, RT])
        stat = sb("stat", [P, 3, TT])
        cL = sb("cL", [P, RT, NCH])
        ident = cst[:, K_ID:K_ID + P]
        ones2 = cst[:, K_ONES2:K_ONES2 + P]

        xs = at(0, TT, D)
        sqj = at(32, D)
        nw = at(36, D)
        AR = at(0, RT, NCH, 2, L)
        BK = at(32, RT, NCH, 2, L)
        V = at(64, RT, T)
        conv_st = at(80, 2, T)
        bonus_st = at(88, 2, T)
        xnT = at(96, KT, T)
        win = at(128, 3, KT * P)
        praw = at(140, 2, 1028)
        q_r, q_k, W1, W2, W3, W4, W6, W7, W8 = (at(149 + 4 * n, T) for n in range(9))
        u_cv = at(140, 1028)
        ccs = at(145, T)
        t_cv = at(149, T)
        tdwa = at(185, T)
        lora = at(189, RW)
        sdg = at(192, T)

        YF = at(96, RT, T)
        CB = 28
        ARc, BKc, BKs, MTb, TTb, Ebd, UTb = (
            [at(128 + CB * s + o, RT, 2, L) for s in range(2)] for o in (0, 2, 4, 6, 8, 10, 12))
        Gm, = ([at(128 + CB * s + o, 2 * RT, 2 * L) for s in range(2)] for o in (14,))
        BKt, SAV = ([at(128 + CB * s + o, 2 * RT, L) for s in range(2)] for o in (18, 20))
        Vc, Tst, Est, NVs = ([at(128 + CB * s + o, RT, L) for s in range(2)] for o in (22, 23, 24, 25))
        MAt = [at(128 + CB * s + 26, 2, RT, L) for s in range(2)]
        St = [at(184 + s, RT, L) for s in range(2)]
        Sc = at(186, RT, L)

        mixT = at(128, 2 * RT, T)
        bonus_in = at(112, RT, T)
        gn_yc, gn_sq, gn_sd = ([at(64 + 12 * s + o, T) for s in range(2)] for o in (0, 4, 8))
        wgate = at(88, RW)
        wo = at(160, KT, D)
        h_sb = at(96, TT, D)
        xres = [at(64 + 4 * s, D) for s in range(2)]
        sqj2 = at(72, D)
        xn2 = [at(76 + 4 * s, D) for s in range(2)]
        xn2T = [at(84 + 4 * s, KT, P) for s in range(2)]
        nw2 = at(92, D)
        rw = at(192, KT, E)
        lg, hot, prod, hots = (at(193 + n * 0.125, E) for n in range(4))
        rk = at(193.5, E)
        hot4 = at(194, TOPK, E)
        rb = at(194.5, E)
        G = at(195, TT, E)
        cst2 = sb("cst2", [P, NCONST - K_MIX])
        tri, ones, iexp, itok = (cst2[:, a - K_MIX:b - K_MIX] for a, b in (
            (K_TRI, K_ALL), (K_ALL, K_EXP), (K_EXP, K_TOK), (K_TOK, NCONST)))
        desc = sb("desc", [P, E])
        eoff = sb("eoff", [P, E])
        seen = sb("seen", [P, E])
        topv = sb("topv", [P, TT, TOPK])
        gates = sb("gates", [P, TT, TOPK])
        small = sb("small", [P, 8])
        gsum = sb("gsum", [P, TT])
        slot_f = sb("slot_f", [P, TOPK])
        slot_i = sb("slot_i", [P, TT, TOPK], I32)
        entry = sb("entry", [P, TT, TOPK, 2], I32)
        flags = sb("flags", [P, 8], I32)
        stat2 = sb("stat2", [P, 3, TT])
        stat3 = sb("stat3", [P, 3, TT])
        wslot = [at(16 * u, KT, HALF) for u in range(6)]
        xg = at(128, D)
        xg2 = at(132, D)
        xT = at(136, KT, C)
        actT = at(141, KT, C)
        yT = at(146, KT, C)
        Yt = at(151, D)
        Y2 = at(155, D)
        gub = at(159, E * 2 * KT)
        gub1 = at(161, E * 2 * KT)
        gt, lt, sgm = ([at(163 + 2 * k + 0.75 * s, C) for s in range(2)] for k in range(3))
        idx_g = sb("idx_g", [P, 2], I32)
        idx_g2 = sb("idx_g2", [P, 2], I32)
        idx_s = sb("idx_s", [P, 2], I32)
        idx_s2 = sb("idx_s2", [P, 2], I32)
        ypair = [at(16 * s, TOPK, D) for s in range(2)]
        dnb = at(40, D)
        GT = at(44, TT, P)
        nw3 = at(48, D)
        sqj3 = at(52, D)
        fin = [at(56 + 4 * s, D) for s in range(2)]

        s_x = [sem(f"x_in{t}") for t in range(2)]
        s_par = sem("params_in")
        s_sq = sem("squares")
        s_ms = sem("mean_square")
        s_rt = sem("root")
        s_xn = sem("x_normalised")
        s_tr = sem("x_transposed")
        s_te = sem("xT_evacuated_act")
        s_tv = sem("xT_evacuated_dve")
        s_w = [sem(f"w_in{k}") for k in range(3)]
        s_pj = sem("projected")
        s_pc = sem("praw_copied")
        s_pu = sem("praw_used")
        s_lo = sem("lora_acts")
        s_pm = sem("prep_products")
        s_sg = sem("sigmoids")
        s_cu = sem("cumulated")
        s_ex = sem("exps")
        s_kk = sem("kk_ready")
        s_sk = sem("kk_squared")
        s_nr = sem("norms")
        s_td = sem("tile_done")
        s_rk = sem("rk_ready")
        s_bu = sem("bonus_made")
        s_bo = [sem(f"bonus_out{k}") for k in range(2)]
        s_dv = sem("dve_step")
        s_ccp = sem("cc_copied")
        s_u = sem("u_made")
        s_cd = sem("conv_done")
        s_cvo = sem("conv_out")
        s_cds = sem("conv_step")
        s_pz = sem("pads_zero")
        s_pcv = sem("conv_projected")
        s_wcv = [sem(f"w_conv{k}") for k in range(3)]

        two = lambda name: [sem(f"{name}{s}") for s in range(2)]
        s_z = sem("chunk_buffers_zero")
        s_zv = sem("state_zero")
        s_st = two("chunk_staged")
        s_bs = sem("BK_scaled")
        s_g, s_m, s_v, s_bt = sem("scores"), sem("M_and_At"), sem("Vt"), sem("BKt")
        s_gm, s_mt, s_tt0 = two("scores_masked"), sem("MT_copied"), two("TT_first")
        s_ac, s_bc = sem("At_copied"), two("BKt_copied")
        s_pe_e, s_pe_f, s_pe_ft = two("E"), two("F"), two("FT")
        s_e, s_t, s_tt = two("E_masked"), two("T_updated"), two("TT_updated")
        s_nv, s_ut, s_nvc, s_utc = sem("NV"), sem("UT"), sem("NV_copied"), sem("UT_copied")
        s_sa, s_sac, s_sn, s_s = sem("SA"), sem("SA_copied"), sem("state_product"), two("state")
        s_y, s_yc = two("Y"), two("Y_copied")
        s_cst = sem("chunk_step")
        s_cvr, s_scr = sem("conv_stage_free"), sem("expert_rows_free")
        s_pe_apart, s_pool_apart = sem("pe_apart"), sem("pool_apart")
        s_pi = sem("post_inputs")
        s_wo = sem("w_out_in")
        s_mp, s_vp, s_gp = sem("mean_product"), sem("var_product"), sem("gate_product")
        s_yc2, s_ysq, s_va, s_sd, s_mix = (sem("y_centred"), sem("y_squared"), sem("var"), sem("deviation"),
                                           sem("mix_ready"))
        s_xr = two("x_again")
        s_op, s_h, s_sq2, s_ms2, s_rt2, s_xn2 = (sem("out_projected"), sem("h_ready"), sem("h_squared"),
                                                 sem("h_mean_square"), sem("h_root"), sem("xn2_ready"))
        s_xw = two("xn2_written")
        s_t2, s_t2c, s_lg, s_lgu = sem("xn2_transposed"), sem("xn2T_copied"), sem("logits"), sem("logits_used")
        s_hot, s_rank, s_rku, s_slot = sem("experts_chosen"), sem("ranks"), sem("ranks_used"), sem("slots")
        s_ls, s_l0 = sem("lists_written"), sem("lists_cleared")
        s_ex2, s_g4, s_flag = sem("gate_shifted"), sem("gate_exp"), sem("flags_ready")
        s_mi = sem("moe_inputs")
        s_wt = [sem(f"expert_w{u}") for u in range(6)]
        s_ig, s_gx, s_is, s_sc = (sem("gather_list_in"), sem("tokens_gathered"), sem("scatter_list_in"),
                                  sem("rows_scattered"))
        s_xt, s_xe, s_gu, s_gd, s_g1, s_gs, s_act = (sem("xT"), sem("xT_copied"), sem("gu"), sem("gu_read"), sem("glu"),
                                                     sem("glu_sigmoid"), sem("act_ready"))
        s_dn, s_dd, s_yt, s_ye, s_l1 = sem("dn"), sem("dn_copied"), sem("y_by_token"), sem("y_rows"), sem("lin")
        s_md, s_gT, s_gTc, s_bp, s_yl = (sem("experts_done"), sem("gates_transposed"), sem("gatesT_copied"),
                                         sem("bias_product"), two("pairs_in"))
        s_fi, s_hf, s_o, s_out = sem("final_inputs"), sem("h_final"), sem("out_ready"), two("written")
        s_fs = sem("final_step")

        NR = 2 + 3 * RT

        def weights_of(e, u):
            src = gu_w if u < 4 else dn_w
            o = u * HALF if u < 4 else (u - 4) * HALF
            return src[bass.ds(e, 1), :, o:o + HALF].rearrange("a (k p) n -> p (a k) n", p=P)

        def rounds(eng, body):
            body(0)
            eng.wait_ge(s_flag, 1)
            with eng.Fori(1, ROUNDS) as r:
                need = eng.value_load(flags[0:1, bass.ds(r, 1)], min_val=0, max_val=1)
                with eng.If(need > 0):
                    body(r)

        block = ctx.enter_context(nc.Block())

        def ring_pair(n):
            return 2 * (n % 3)

        @block.sync
        def _(sp):
            sp.dma_start(cst[:, :], consts_d[:, 0:K_MIX]).then_inc(s_par, 16)
            for t in range(2):
                sp.dma_start(xs[:, 4 * t:4 * t + 4, :], x[4 * t * P:4 * (t + 1) * P, :].rearrange("(t p) n -> p t n", p=P)
                             ).then_inc(s_x[t], 16)
            sp.dma_start(nw, normw_d[0]).then_inc(s_par, 16)
            sp.dma_start(prm[:, :], prm_d).then_inc(s_par, 16)
            sp.dma_start(lora, lora_d).then_inc(s_par, 16)
            for n in range(NR):
                if n >= 3:
                    sp.wait_ge(s_pj, 2 * (n - 2))
                sp.dma_start(win[:, n % 3, :], w_in_t[n]).then_inc(s_w[n % 3], 16)
            for j in range(3):
                sp.wait_ge(s_pj, 2 * (NR + j - 2))
                sp.dma_start(win[:, (NR + j) % 3, :], w_in_t[NR + j]).then_inc(s_wcv[j], 16)
            with sp.Fori(1, RT) as i:
                for j in range(3):
                    sp.wait_ge(s_pcv, 6 * i + 2 * j - 4)
                    sp.dma_start(win[:, (NR + j) % 3, :],
                                 w_in_t[bass.ds(NR + 3 * i + j, 1)].rearrange("a p n -> (a p) n")
                                 ).then_inc(s_wcv[j], 16)

            sp.wait_ge(s_z, 2)
            with sp.Fori(0, NCH // 2) as it:
                for s in range(2):
                    c = 2 * it + s
                    sp.wait_ge(s_y[s], it + 1)
                    sp.dma_start(ARc[s], AR[:, :, bass.ds(c, 1), :, :].rearrange("p r c k t -> p (r c) k t")
                                 ).then_inc(s_st[s], 16)
                    sp.dma_start(BKc[s], BK[:, :, bass.ds(c, 1), :, :].rearrange("p r c k t -> p (r c) k t")
                                 ).then_inc(s_st[s], 16)
                    sp.dma_start(Vc[s], V[:, :, bass.ds(c * L, L)]).then_inc(s_st[s], 16)

            sp.wait_ge(s_yc[0], NCH // 2 + 1)
            sp.wait_ge(s_yc[1], NCH // 2 + 1)
            sp.wait_ge(s_s[1], NCH // 2 + 1)
            for i in range(RT):
                sp.dma_start(bonus_in[:, i, :], bonus_d[i]).then_inc(s_pi, 16)
            sp.dma_start(wgate, wgate_d).then_inc(s_pi, 16)
            for i in range(RT):
                sp.dma_start(mixT[:, i, :], conv_d[i]).then_inc(s_wo, 16)
            sp.dma_start(wo, w_out.rearrange("(k p) n -> p k n", p=P)).then_inc(s_wo, 16)
            sp.dma_start(cst2[:, :], consts_d[:, K_MIX:NCONST]).then_inc(s_wo, 16)
            for u in range(4):
                sp.dma_start(wslot[u], weights_of(0, u)).then_inc(s_wt[u], 16)
            sp.wait_ge(s_mix, RT)
            sp.dma_start(rw, router_w.rearrange("(k p) n -> p k n", p=P)).then_inc(s_mi, 16)
            sp.dma_start(rb, router_b).then_inc(s_mi, 16)
            sp.dma_start(nw2, normw_d[1]).then_inc(s_mi, 16)
            for t in range(TT):
                if t >= 2:
                    sp.wait_ge(s_h, t - 1)
                sp.dma_start(xres[t % 2], x[t * P:(t + 1) * P, :]).then_inc(s_xr[t % 2], 16)
                if t:
                    sp.wait_ge(s_xn2, t)
                    sp.dma_start(xn_d[(t - 1) * P:t * P, :], xn2[(t - 1) % 2]).then_inc(s_xw[(t - 1) % 2], 16)
            sp.wait_ge(s_xn2, TT)
            sp.dma_start(xn_d[(TT - 1) * P:T, :], xn2[(TT - 1) % 2]).then_inc(s_xw[(TT - 1) % 2], 16)
            sp.wait_ge(s_lg, TT)
            sp.dma_start(gub, gub_d).then_inc(s_mi, 16)
            sp.wait_ge(s_xw[0], 16 * TT // 2)
            sp.wait_ge(s_xw[1], 16 * TT // 2)
            for u in (4, 5):
                sp.dma_start(wslot[u], weights_of(0, u)).then_inc(s_wt[u], 16)

            def expert_weights(lo, r):
                with sp.Fori(lo, E) as e:
                    for u in range(6):
                        n = r * E + e
                        if u < 4:
                            sp.wait_ge(s_gu, 8 * n + 2 * u - 6)
                        else:
                            sp.wait_ge(s_dn, 8 * n + 4 * u - 20)
                        sp.dma_start(wslot[u], weights_of(e, u)).then_inc(s_wt[u], 16)

            rounds(sp, lambda r: expert_weights(1 if isinstance(r, int) else 0, r))

            sp.wait_ge(s_md, 1)
            sp.dma_start(dnb[0:E, :], dn_b).then_inc(s_fi, 16)
            sp.dma_start(nw3, normw_d[2]).then_inc(s_fi, 16)
            pairs = pair_d.rearrange("(k t) n -> t k n", k=TOPK)
            for t in range(TT + 1):
                if t < TT:
                    if t >= 2:
                        sp.wait_ge(s_hf, t - 1)
                    sp.dma_start(ypair[t % 2], pairs[t * P:(t + 1) * P]).then_inc(s_yl[t % 2], 16)
                if t >= 1:
                    sp.wait_ge(s_o, t)
                    sp.dma_start(out[(t - 1) * P:t * P, :], fin[(t - 1) % 2]).then_inc(s_out[(t - 1) % 2], 16)
            for k in range(2):
                sp.wait_ge(s_out[k], 16 * TT // 2)

        @block.gpsimd
        def _(pool):
            for ahead in (*s_y, *s_yc, *s_s, s_ccp, s_u, s_cd, s_cvr, s_scr, s_ye):
                pool.sem_inc(ahead, 1)
            pool.dma_start(list_d, list0_d).then_inc(s_l0, 16)
            nc.gpsimd.memset(praw[:, :, 0:1], 0.0).then_inc(s_pz, 1)
            for i in range(RT - 1):
                pool.wait_ge(s_bu, i + 1)
                pool.dma_start(bonus_d[i], bonus_st[:, i % 2, :]).then_inc(s_bo[i % 2], 16)
            with pool.Fori(0, RT) as i:
                pool.wait_ge(s_cd, 2 * i + 3)
                pool.dma_start(conv_d[bass.ds(i, 1)].rearrange("a p n -> (a p) n"), conv_st[:, 0, :]).then_inc(s_cvo, 16)
                pool.wait_ge(s_cvo, 16 * i + 16)
                pool.sem_inc(s_cvr, 1)
            pool.wait_ge(s_bu, RT)
            pool.dma_start(bonus_d[RT - 1], bonus_st[:, (RT - 1) % 2, :]).then_inc(s_bo[(RT - 1) % 2], 16)
            for k in range(2):
                pool.wait_ge(s_bo[k], 16 * RT // 2)
            for s in range(2):
                for b in (MTb[s], UTb[s]):
                    last = nc.gpsimd.memset(b, 0.0)
                last.then_inc(s_z, 1)
            pool.wait_ge(s_z, 2)
            bd1 = cst[:, K_BD:K_BD + P].rearrange("p (k t) -> p k t", t=L).unsqueeze(1).to_broadcast([P, RT, 2, L])
            idb = ident.rearrange("p (k t) -> p k t", t=L).unsqueeze(1).to_broadcast([P, RT, 2, L])
            with pool.Fori(0, NCH // 2) as it:
                for s in range(2):
                    pool.wait_ge(s_mt, 2 * it + s + 1)
                    nc.gpsimd.tensor_tensor(TTb[s], MTb[s], bd1, ALU.mult).then_inc(s_tt0[s], 1)
                    pool.wait_ge(s_tt0[s], 2 * it + 1)
                    nc.gpsimd.tensor_tensor(TTb[s], TTb[s], idb, ALU.add).then_inc(s_tt0[s], 1)
            pool.wait_ge(s_l0, 16)
            for t in range(TT):
                pool.wait_ge(s_slot, t + 1)
                for k in range(TOPK):
                    pool.indirect_dma_start(list_d, bass.IndirectOffsetOnAxis(ap=slot_i[:, t, k:k + 1], axis=0),
                                            entry[:, t, k, :], None).then_inc(s_ls, 16)
            pool.wait_ge(s_ls, 16 * TT * TOPK)
            for k in range(2):
                pool.wait_ge(s_xw[k], 16 * TT // 2)
            pool.wait_ge(s_lg, TT)

            def list_in(e, r, big, little, sem_in):
                o = e * LIST + r * C
                pool.dma_start(big[:, :], list_d[bass.ds(o, P), :]).then_inc(sem_in, 16)
                pool.dma_start(little[0:C2, :], list_d[bass.ds(o + P, C2), :]).then_inc(sem_in, 16)

            def gather(e, r, m):
                pool.wait_ge(s_gx, 32 * m)
                pool.sem_inc(s_pool_apart, 1)
                list_in(e, r, idx_g, idx_g2, s_ig)
                pool.wait_ge(s_ig, 32 * m + 32)
                pool.wait_ge(s_xt, 4 * m)
                pool.sem_inc(s_pool_apart, 1)
                pool.indirect_dma_start(xg, None, xn_d, bass.IndirectOffsetOnAxis(ap=idx_g[:, 0:1], axis=0)
                                        ).then_inc(s_gx, 16)
                pool.indirect_dma_start(xg2[0:C2, :], None, xn_d,
                                        bass.IndirectOffsetOnAxis(ap=idx_g2[0:C2, 0:1], axis=0)).then_inc(s_gx, 16)

            def expert_rows(r):
                gather(0, r, r * (E + 1))
                with pool.Fori(0, E) as e:
                    n = r * E + e
                    gather(e + 1, r, r * (E + 1) + e + 1)
                    list_in(e, r, idx_s, idx_s2, s_is)
                    pool.wait_ge(s_is, 32 * n + 32)
                    pool.wait_ge(s_ye, 4 * n + 5)
                    pool.sem_inc(s_pool_apart, 1)
                    pool.indirect_dma_start(pair_d, bass.IndirectOffsetOnAxis(ap=idx_s[:, 1:2], axis=0), Yt, None,
                                            bounds_check=PAIRS - 1, oob_is_err=False).then_inc(s_sc, 16)
                    pool.indirect_dma_start(pair_d, bass.IndirectOffsetOnAxis(ap=idx_s2[0:C2, 1:2], axis=0), Y2[0:C2, :],
                                            None, bounds_check=PAIRS - 1, oob_is_err=False).then_inc(s_sc, 16)
                    pool.wait_ge(s_sc, 32 * n + 32)
                    pool.sem_inc(s_scr, 1)

            rounds(pool, expert_rows)
            pool.sem_inc(s_md, 1)

        @block.scalar
        def _(act):
            for t in range(TT):
                act.wait_ge(s_x[t // 4], 16)
                if t:
                    act.wait_ge(s_sq, t)
                nc.scalar.activation(sqj, xs[:, t, :], ACT.Square, accum_out=stat[:, 0, t:t + 1]).then_inc(s_sq, 1)
            act.wait_ge(s_ms, 1)
            nc.scalar.activation(stat[:, 1, :], stat[:, 1, :], ACT.Sqrt).then_inc(s_rt, 1)
            for t in range(TT):
                act.wait_ge(s_tr, 2 * t + 1)
                nc.scalar.copy(xnT[:, 0:4, t * P:(t + 1) * P],
                               ps[:, 2 * (t % 2), :].rearrange("p (k t) -> p k t", t=P)).then_inc(s_te, 1)
            def copy_raw(n):
                for h in range(2):
                    act.wait_ge(s_pj, 2 * n + h + 1)
                    if h == 0 and n >= 2:
                        act.wait_ge(s_pu, n - 1)
                    nc.scalar.copy(praw[:, n % 2, 1 + h * HALF:1 + (h + 1) * HALF],
                                   ps[:, ring_pair(n) + h, :]).then_inc(s_pc, 1)
            copy_raw(0)
            copy_raw(1)
            act.wait_ge(s_pu, 1)
            nc.scalar.activation(tdwa[0:LORA, :], tdwa[0:LORA, :], ACT.Tanh).then_inc(s_lo, 1)
            act.wait_ge(s_pu, 2)
            nc.scalar.activation(sdg, sdg, ACT.Sigmoid).then_inc(s_lo, 1)
            for i in range(RT):
                n = 2 + 3 * i
                copy_raw(n)
                for h in range(2):
                    act.wait_ge(s_pm, 8 * i + h + 1)
                    if h == 0 and i:
                        act.wait_ge(s_td, i)
                    nc.scalar.activation(W1[:, h * HALF:(h + 1) * HALF], ps[:, 6 + h, :], ACT.Sigmoid,
                                         bias=prm[:, W0 + i:W0 + i + 1]).then_inc(s_sg, 1)
                copy_raw(n + 1)
                for h in range(2):
                    act.wait_ge(s_pm, 8 * i + 2 + h + 1)
                    nc.scalar.activation(W4[:, h * HALF:(h + 1) * HALF], ps[:, 6 + h, :], ACT.Sigmoid,
                                         bias=prm[:, A0 + i:A0 + i + 1]).then_inc(s_sg, 1)
                act.wait_ge(s_cu, i + 1)
                nc.scalar.activation(W3, W2, ACT.Exp, scale=-KAPPA).then_inc(s_ex, 1)
                nc.scalar.activation(W1, W1, ACT.Exp, scale=-KAPPA).then_inc(s_ex, 1)
                act.wait_ge(s_ex, 3 * i + 1)
                nc.scalar.activation(W2, W2, ACT.Exp, scale=KAPPA).then_inc(s_ex, 1)
                act.wait_ge(s_kk, i + 1)
                if i:
                    act.wait_ge(s_bu, i)
                nc.scalar.activation(W8, W7, ACT.Square).then_inc(s_sk, 1)
                copy_raw(n + 2)
                for h in range(2):
                    act.wait_ge(s_pm, 8 * i + 4 + h + 1)
                    nc.scalar.activation(W8[:, h * HALF:(h + 1) * HALF], ps[:, 6 + h, :], ACT.Sqrt).then_inc(s_nr, 1)
            with act.Fori(0, RT) as i:
                for h in range(2):
                    act.wait_ge(s_pcv, 6 * i + h + 1)
                    if h == 0:
                        act.wait_ge(s_u, 2 * i + 1)
                        act.wait_ge(s_td, RT)
                        act.wait_ge(s_pu, NR)
                    nc.scalar.copy(ccs[:, h * HALF:(h + 1) * HALF], ps[:, ring_pair(NR) + h, :]).then_inc(s_ccp, 1)

            lo, hi = slice(0, N), slice(N, P)
            act.wait_ge(s_z, 2)
            with act.Fori(0, NCH // 2) as it:
                for s in range(2):
                    b = 4 * s
                    act.wait_ge(s_gm[s], 2 * it + 2)
                    gm = Gm[s].rearrange("p (r h) q -> p r h q", h=2)
                    nc.scalar.copy(MTb[s][lo, :, 0, :], gm[lo, :, 0, 0:L])
                    nc.scalar.copy(MTb[s][hi, :, 1, :], gm[hi, :, 1, 0:L]).then_inc(s_mt, 1)
                    act.wait_ge(s_v, 2 * it + s + 1)
                    vq = ps[:, b + 3, 0:RT * L].rearrange("p (r i) -> p r i", i=L)
                    sv = SAV[s].rearrange("p (r h) i -> p r h i", h=2)
                    nc.scalar.copy(sv[hi, :, 0, :], vq[hi])
                    nc.scalar.copy(sv[lo, :, 1, :], vq[lo])
                    act.wait_ge(s_m, 2 * it + s + 1)
                    nc.scalar.copy(MAt[s], ps[:, b + 2, :].rearrange("p (k r i) -> p k r i", k=2, r=RT)
                                   ).then_inc(s_ac, 1)
                for s in range(2):
                    act.wait_ge(s_bt, 2 * it + s + 1)
                    bt = BKt[s].rearrange("p (r h) i -> p r h i", h=2)
                    for h in range(2):
                        nc.scalar.copy(bt[:, :, h, :], ps[:, 4 * s + 3 - h, 0:RT * L].rearrange("p (r i) -> p r i", i=L)
                                       ).then_inc(s_bc[s], 1)
                for s in range(2):
                    b = 4 * s
                    act.wait_ge(s_nv, 2 * it + s + 1)
                    nc.scalar.copy(NVs[s], ps[:, b + 3, 0:RT * L].rearrange("p (r i) -> p r i", i=L)).then_inc(s_nvc, 1)
                for s in range(2):
                    b = 4 * s
                    act.wait_ge(s_ut, 2 * it + s + 1)
                    uq = ps[:, b + 3, 0:RT * L].rearrange("p (r i) -> p r i", i=L)
                    nc.scalar.copy(UTb[s][lo, :, 0, :], uq[lo])
                    nc.scalar.copy(UTb[s][hi, :, 1, :], uq[hi]).then_inc(s_utc, 1)
                for s in range(2):
                    act.wait_ge(s_y[s], it + 2)
                    nc.scalar.copy(YF[:, :, bass.ds((2 * it + s) * L, L)],
                                   ps[:, 4 * s + 1, 0:RT * L].rearrange("p (r i) -> p r i", i=L)).then_inc(s_yc[s], 1)
            for i in range(RT):
                act.wait_ge(s_yc2, 2 * i + 2)
                nc.scalar.activation(gn_sq[i % 2], gn_yc[i % 2], ACT.Square).then_inc(s_ysq, 1)
                act.wait_ge(s_va, 2 * i + 2)
                nc.scalar.activation(gn_sd[i % 2], gn_sd[i % 2], ACT.Sqrt).then_inc(s_sd, 1)
            for t in range(TT + 1):
                if t < TT:
                    act.wait_ge(s_h, t + 1)
                    if t:
                        act.wait_ge(s_sq2, t)
                    nc.scalar.activation(sqj2, h_sb[:, t, :], ACT.Square, accum_out=stat2[:, 0, t:t + 1]
                                         ).then_inc(s_sq2, 1)
                    act.wait_ge(s_ms2, t + 1)
                    nc.scalar.activation(stat2[:, 1, t:t + 1], stat2[:, 1, t:t + 1], ACT.Sqrt).then_inc(s_rt2, 1)
                if t:
                    u = t - 1
                    for g in range(2):
                        act.wait_ge(s_t2, 2 * u + g + 1)
                        nc.scalar.copy(xn2T[u % 2][:, 4 * g:4 * g + 4, :],
                                       ps[:, 4 + g, :].rearrange("p (k t) -> p k t", t=P)).then_inc(s_t2c, 1)
                    act.wait_ge(s_ex2, t)
                    nc.scalar.activation(gates[:, u, :], gates[:, u, :], ACT.Exp, accum_out=gsum[:, u:u + 1]
                                         ).then_inc(s_g4, 1)

            def copy_xT(m):
                for q in range(4):
                    act.wait_ge(s_xt, 4 * m + q + 1)
                    nc.scalar.copy(xT[:, 2 * q:2 * q + 2, :], ps[:, 4 + q % 2, 0:2 * C].rearrange("p (k c) -> p k c", c=C)
                                   ).then_inc(s_xe, 1)

            def expert_act(r):
                copy_xT(r * (E + 1))
                with act.Fori(0, E) as e:
                    n = r * E + e
                    for f in range(KT):
                        act.wait_ge(s_g1, 8 * n + f + 1)
                        nc.scalar.activation(sgm[f % 2], gt[f % 2], ACT.Sigmoid, scale=ALPHA).then_inc(s_gs, 1)
                    copy_xT(r * (E + 1) + e + 1)
                    for d in range(KT):
                        act.wait_ge(s_dn, 8 * n + d + 1)
                        nc.scalar.copy(yT[:, d, :], ps[:, 2 + d % 2, 0:C]).then_inc(s_dd, 1)

            rounds(act, expert_act)
            act.wait_ge(s_md, 1)
            act.wait_ge(s_gT, 1)
            nc.scalar.copy(GT[0:E, 0:4, :], ps[0:E, 0, :].rearrange("p (k t) -> p k t", t=P))
            nc.scalar.copy(GT[0:E, 4:8, :], ps[0:E, 1, :].rearrange("p (k t) -> p k t", t=P)).then_inc(s_gTc, 1)
            for t in range(TT):
                act.wait_ge(s_hf, t + 1)
                act.wait_ge(s_sq2, TT + t)
                nc.scalar.activation(sqj3, h_sb[:, t, :], ACT.Square, accum_out=stat3[:, 0, t:t + 1]).then_inc(s_sq2, 1)
                act.wait_ge(s_ms2, TT + t + 1)
                nc.scalar.activation(stat3[:, 1, t:t + 1], stat3[:, 1, t:t + 1], ACT.Sqrt).then_inc(s_rt2, 1)

        @block.vector
        def _(dve):
            ch = Chain(dve, s_dv)
            dve.wait_ge(s_sq, TT)
            nc.vector.tensor_scalar(stat[:, 1, :], stat[:, 0, :], 1.0 / D, RMS_EPS, ALU.mult, ALU.add).then_inc(s_ms, 1)
            dve.wait_ge(s_rt, 1)
            ch.link(nc.vector.reciprocal(stat[:, 2, :], stat[:, 1, :]))
            dve.wait_ge(s_par, 4 * 16)
            for t in range(TT):
                nc.vector.scalar_tensor_tensor(out=xs[:, t, :], in0=xs[:, t, :], scalar=stat[:, 2, t:t + 1],
                                               in1=nw, op0=ALU.mult, op1=ALU.mult).then_inc(s_xn, 1)
            for t in range(TT):
                dve.wait_ge(s_tr, 2 * t + 2)
                nc.vector.tensor_copy(xnT[:, 4:8, t * P:(t + 1) * P],
                                      ps[:, 2 * (t % 2) + 1, :].rearrange("p (k t) -> p k t", t=P)).then_inc(s_tv, 1)
            ch.link(nc.vector.tensor_scalar(omka[:, :], prm[:, KAW:KAW + RT], -1.0, 1.0, ALU.mult, ALU.add))

            def shift(n, dst, wait=None):
                dve.wait_ge(s_pc, 2 * n + 2)
                if n == 0:
                    dve.wait_ge(s_pz, 1)
                now, past = praw[:, n % 2, 1:1 + T], praw[:, n % 2, 0:T]
                ch.link(nc.vector.tensor_tensor(W6, past, now, ALU.subtract))
                mu = {0: 12, 1: 13}.get(n, (n - 2) % 3 * RT + (n - 2) // 3)
                nc.vector.scalar_tensor_tensor(out=dst, in0=W6, scalar=prm[:, MU + mu:MU + mu + 1], in1=now,
                                               op0=ALU.mult, op1=ALU.add).then_inc(s_pu, 1)
                dve.wait_ge(s_pu, n + 1)

            shift(0, tdwa)
            shift(1, sdg)

            def bonus_product(i):
                dve.wait_ge(s_pm, 8 * i + 8)
                if i >= 2:
                    dve.wait_ge(s_bo[i % 2], 16 * (i // 2))
                nc.vector.tensor_tensor(bonus_st[:, i % 2, 0:HALF], ps[:, 6, :], V[:, i, 0:HALF], ALU.mult)
                nc.vector.tensor_tensor(bonus_st[:, i % 2, HALF:T], ps[:, 7, :], V[:, i, HALF:T],
                                        ALU.mult).then_inc(s_bu, 1)

            for i in range(RT):
                n = 2 + 3 * i
                if i:
                    bonus_product(i - 1)
                shift(n, q_r)
                dve.wait_ge(s_sg, 4 * i + 2)
                for c in range(NCH):
                    w = slice(c * L, (c + 1) * L)
                    last = nc.vector.tensor_tensor_scan(W2[:, w], W1[:, w], W1[:, w], 0.0, ALU.add, ALU.max)
                ch.link(last)
                nc.vector.tensor_tensor(W1, W2, W1, ALU.subtract).then_inc(s_cu, 1)
                shift(n + 1, q_k)
                nc.vector.tensor_scalar(W7, q_k, prm[:, KKW + i:KKW + i + 1], None, ALU.mult).then_inc(s_kk, 1)
                dve.wait_ge(s_ex, 3 * i + 1)
                nc.vector.tensor_tensor(AR[:, i, :, 1, :], q_r.rearrange("p (c t) -> p c t", t=L),
                                        W3.rearrange("p (c t) -> p c t", t=L), ALU.mult)
                nc.vector.tensor_copy(cL[:, i, :], W3.rearrange("p (c t) -> p c t", t=L)[:, :, L - 1])
                dve.wait_ge(s_sg, 4 * i + 4)
                ch.link(nc.vector.tensor_scalar(W6, W4, prm[:, KAW + i:KAW + i + 1], omka[:, i:i + 1], ALU.mult, ALU.add))
                ch.link(nc.vector.tensor_tensor(q_k, q_k, W6, ALU.mult))
                dve.wait_ge(s_ex, 3 * i + 3)
                cv = [a.rearrange("p (c t) -> p c t", t=L) for a in (W4, q_k, W2, W1, W7)]
                lo, hi = slice(0, N), slice(N, P)
                nc.vector.tensor_tensor(BK[lo, i, :, 1, :], cv[1][lo], cv[2][lo], ALU.mult)
                nc.vector.tensor_tensor(BK[hi, i, :, 0, :], cv[1][hi], cv[2][hi], ALU.mult)
                dve.wait_ge(s_nr, 2 * i + 2)
                ch.link(nc.vector.tensor_scalar(W8, W8, 1e-12, None, ALU.max))
                ch.link(nc.vector.reciprocal(W8, W8))
                ch.link(nc.vector.tensor_tensor(W7, W7, W8, ALU.mult))
                ch.link(nc.vector.tensor_tensor(W4, W4, W7, ALU.mult))
                nc.vector.scalar_tensor_tensor(out=W8, in0=q_r, scalar=prm[:, RKW + i:RKW + i + 1], in1=q_k,
                                               op0=ALU.mult, op1=ALU.mult).then_inc(s_rk, 1)
                nc.vector.tensor_tensor(BK[lo, i, :, 0, :], cv[0][lo], cv[2][lo], ALU.mult)
                nc.vector.tensor_tensor(BK[hi, i, :, 1, :], cv[0][hi], cv[2][hi], ALU.mult)
                nc.vector.scalar_tensor_tensor(out=AR[:, i, :, 0, :], in0=cv[4], scalar=-1.0, in1=cv[3],
                                               op0=ALU.mult, op1=ALU.mult).then_inc(s_td, 1)
                shift(n + 2, V[:, i, :])
            ch.link(nc.vector.memset(u_cv[:, 0:2], 0.0))
            with dve.Fori(0, RT) as i:
                cc = Chain(dve, s_cds, i * 3)
                w = [prm[:, bass.ds(CVW + i * 3 + j, 1)] for j in range(3)]
                for h in range(2):
                    dve.wait_ge(s_ccp, 2 * i + h + 2)
                    dve.wait_ge(s_pcv, 6 * i + 2 + h + 1)
                    nc.vector.tensor_tensor(u_cv[:, 2 + h * HALF:2 + (h + 1) * HALF], ccs[:, h * HALF:(h + 1) * HALF],
                                            ps[:, ring_pair(NR + 1) + h, :], ALU.mult).then_inc(s_u, 1)
                dve.wait_ge(s_u, 2 * i + 3)
                cc.link(nc.vector.tensor_scalar(t_cv, u_cv[:, 0:T], w[0], None, ALU.mult))
                cc.link(nc.vector.scalar_tensor_tensor(out=t_cv, in0=u_cv[:, 1:1 + T], scalar=w[1], in1=t_cv,
                                                       op0=ALU.mult, op1=ALU.add))
                cc.link(nc.vector.scalar_tensor_tensor(out=t_cv, in0=u_cv[:, 2:2 + T], scalar=w[2], in1=t_cv,
                                                       op0=ALU.mult, op1=ALU.add))
                for h in range(2):
                    dve.wait_ge(s_pcv, 6 * i + 4 + h + 1)
                    dve.wait_ge(s_cvr, i + 1)
                    nc.vector.tensor_tensor(conv_st[:, 0, h * HALF:(h + 1) * HALF], t_cv[:, h * HALF:(h + 1) * HALF],
                                            ps[:, ring_pair(NR + 2) + h, :], ALU.mult).then_inc(s_cd, 1)
            bonus_product(RT - 1)

            lo, hi = slice(0, N), slice(N, P)
            dve.wait_ge(s_z, 2)
            nc.vector.memset(St[0], 0.0).then_inc(s_zv, 1)
            dve.wait_ge(s_zv, 1)
            mg = cst[:, K_MG:K_MG + P].unsqueeze(1).to_broadcast([P, RT, P])
            m1 = cst[:, K_M1:K_M1 + L].unsqueeze(1).to_broadcast([P, RT, L])
            i2 = cst[:, K_ID2:K_ID2 + L].unsqueeze(1).to_broadcast([P, RT, L])
            with dve.Fori(0, NCH // 2) as it:
                cc = Chain(dve, s_cst, it * 2)
                for s in range(2):
                    b = 4 * s
                    dve.wait_ge(s_st[s], 48 * it + 48)
                    if s == 0:
                        dve.wait_ge(s_s[1], it + 1)
                    decay = cL[:, :, bass.ds(2 * it + s, 1)].unsqueeze(3).to_broadcast([P, RT, 1, 2 * L])
                    nc.vector.tensor_tensor(BKs[s].rearrange("p r k t -> p r (k t)").unsqueeze(2),
                                            BKc[s].rearrange("p r k t -> p r (k t)").unsqueeze(2),
                                            decay, ALU.mult).then_inc(s_bs, 1)
                    dve.wait_ge(s_g, 2 * it + s + 1)
                    for g in range(2):
                        nc.vector.tensor_tensor(Gm[s].rearrange("p (r h) q -> p h r q", h=2)[:, g, :, :],
                                                ps[:, b + g, :].rearrange("p (h q) -> p h q", q=P), mg,
                                                ALU.mult).then_inc(s_gm[s], 1)
                    dve.wait_ge(s_ac, 2 * it + s + 1)
                    cc.link(nc.vector.tensor_tensor(Tst[s], MAt[s][:, 0], m1, ALU.mult))
                    nc.vector.tensor_tensor(Tst[s], Tst[s], i2, ALU.add).then_inc(s_t[s], 1)
                for l in range(len(LEVELS)):
                    me = cst[:, K_ME + l * L:K_ME + (l + 1) * L].unsqueeze(1).to_broadcast([P, RT, L])
                    mb = (cst[:, K_MTB + l * P:K_MTB + (l + 1) * P].rearrange("p (k t) -> p k t", t=L)
                          .unsqueeze(1).to_broadcast([P, RT, 2, L]))
                    for s in range(2):
                        b = 4 * s
                        eq = ps[:, b, 0:RT * L].rearrange("p (r i) -> p r i", i=L)
                        dve.wait_ge(s_pe_e[s], 5 * it + l + 1)
                        nc.vector.tensor_tensor(Est[s], eq, me, ALU.mult).then_inc(s_e[s], 1)
                        nc.vector.tensor_tensor(Ebd[s], eq.unsqueeze(2).to_broadcast([P, RT, 2, L]), mb,
                                                ALU.mult).then_inc(s_e[s], 1)
                    for s in range(2):
                        b = 4 * s
                        if l < 4:
                            dve.wait_ge(s_pe_f[s], 4 * it + l + 1)
                            dve.wait_ge(s_t[s], 5 * it + l + 1)
                            nc.vector.tensor_tensor(Tst[s], ps[:, b + 2, 0:RT * L].rearrange("p (r i) -> p r i", i=L),
                                                    Tst[s], ALU.add).then_inc(s_t[s], 1)
                        dve.wait_ge(s_pe_ft[s], 5 * it + l + 1)
                        if l:
                            dve.wait_ge(s_tt[s], 5 * it + l)
                        else:
                            dve.wait_ge(s_tt0[s], 2 * it + 2)
                        nc.vector.tensor_tensor(TTb[s], ps[:, b + 1, :].rearrange("p (r k t) -> p r k t", k=2, t=L),
                                                TTb[s], ALU.add).then_inc(s_tt[s], 1)
                for s in range(2):
                    b = 4 * s
                    if s == 0:
                        dve.wait_ge(s_s[1], it + 1)
                    else:
                        dve.wait_ge(s_s[0], it + 2)
                    decay = cL[:, :, bass.ds(2 * it + s, 1)].to_broadcast([P, RT, L])
                    nc.vector.tensor_tensor(Sc, St[s], decay, ALU.mult).then_inc(s_zv, 1)
                    dve.wait_ge(s_sa, 2 * it + s + 1)
                    aq = ps[:, b + 2, 0:RT * L].rearrange("p (r i) -> p r i", i=L)
                    sv = SAV[s].rearrange("p (r h) i -> p r h i", h=2)
                    nc.vector.tensor_copy(sv[lo, :, 0, :], aq[lo])
                    nc.vector.tensor_copy(sv[hi, :, 1, :], aq[hi]).then_inc(s_sac, 1)
                    dve.wait_ge(s_zv, 2 * it + s + 2)
                    dve.wait_ge(s_sn, 2 * it + s + 1)
                    if s == 1:
                        dve.wait_ge(s_y[0], it + 2)
                    else:
                        dve.wait_ge(s_y[1], it + 1)
                    nc.vector.tensor_tensor(St[1 - s], ps[:, b + 3, 0:RT * L].rearrange("p (r i) -> p r i", i=L),
                                            Sc, ALU.add).then_inc(s_s[s], 1)

            dve.wait_ge(s_pi, 16 * (RT + 1))
            for i in range(RT):
                yc, sd = gn_yc[i % 2], gn_sd[i % 2]
                for h in range(2):
                    w = slice(h * HALF, (h + 1) * HALF)
                    dve.wait_ge(s_mp, 2 * i + h + 1)
                    nc.vector.scalar_tensor_tensor(out=yc[:, w], in0=ps[:, h, :], scalar=-1.0 / N, in1=YF[:, i, w],
                                                   op0=ALU.mult, op1=ALU.add).then_inc(s_yc2, 1)
                for h in range(2):
                    w = slice(h * HALF, (h + 1) * HALF)
                    dve.wait_ge(s_vp, 2 * i + h + 1)
                    nc.vector.tensor_scalar(sd[:, w], ps[:, 2 + h, :], 1.0 / N, GN_EPS, ALU.mult, ALU.add
                                            ).then_inc(s_va, 1)
                dve.wait_ge(s_sd, i + 1)
                ch.link(nc.vector.reciprocal(sd, sd))
                ch.link(nc.vector.tensor_tensor(yc, yc, sd, ALU.mult))
                ch.link(nc.vector.tensor_scalar(yc, yc, prm[:, LNW + i:LNW + i + 1], prm[:, LNB + i:LNB + i + 1],
                                                ALU.mult, ALU.add))
                ch.link(nc.vector.tensor_tensor(yc, yc, bonus_in[:, i, :], ALU.add))
                dve.wait_ge(s_gp, 2 * i + 2)
                nc.vector.tensor_tensor(mixT[:, RT + i, 0:HALF], yc[:, 0:HALF], ps[:, 4, :], ALU.mult)
                nc.vector.tensor_tensor(mixT[:, RT + i, HALF:T], yc[:, HALF:T], ps[:, 5, :], ALU.mult).then_inc(s_mix, 1)

            dve.wait_ge(s_wo, 16 * (RT + 2))
            dve.wait_ge(s_mi, 3 * 16)
            ch.link(nc.vector.memset(seen[:, :], 0.0))
            ch.link(nc.vector.tensor_scalar(desc[:, :], iexp, -1.0, float(E), ALU.mult, ALU.add))
            ch.link(nc.vector.tensor_scalar(eoff[:, :], iexp, float(LIST), None, ALU.mult))
            big = [P, E]
            for t in range(TT + 1):
                if t < TT:
                    dve.wait_ge(s_xr[t % 2], 16 * (t // 2 + 1))
                    dve.wait_ge(s_op, 2 * t + 2)
                    b = 2 * (t % 2)
                    nc.vector.tensor_tensor(h_sb[:, t, 0:HALF], ps[:, b, :], xres[t % 2][:, 0:HALF], ALU.add)
                    nc.vector.tensor_tensor(h_sb[:, t, HALF:D], ps[:, b + 1, :], xres[t % 2][:, HALF:D],
                                            ALU.add).then_inc(s_h, 1)
                    dve.wait_ge(s_sq2, t + 1)
                    nc.vector.tensor_scalar(stat2[:, 1, t:t + 1], stat2[:, 0, t:t + 1], 1.0 / D, RMS_EPS,
                                            ALU.mult, ALU.add).then_inc(s_ms2, 1)
                    dve.wait_ge(s_rt2, t + 1)
                    ch.link(nc.vector.reciprocal(stat2[:, 2, t:t + 1], stat2[:, 1, t:t + 1]))
                    if t >= 2:
                        dve.wait_ge(s_xw[t % 2], 16 * (t // 2))
                        dve.wait_ge(s_t2, 2 * t - 2)
                    nc.vector.scalar_tensor_tensor(out=xn2[t % 2], in0=h_sb[:, t, :], scalar=stat2[:, 2, t:t + 1],
                                                   in1=nw2, op0=ALU.mult, op1=ALU.mult).then_inc(s_xn2, 1)
                if t:
                    u = t - 1
                    dve.wait_ge(s_lg, u + 1)
                    nc.vector.tensor_tensor(lg, ps[:, 6, 0:E], rb, ALU.add).then_inc(s_lgu, 1)
                    dve.wait_ge(s_lgu, u + 1)
                    for k in range(TOPK):
                        ch.link(nc.vector.reduce_max(topv[:, u, k:k + 1], lg, AX.X))
                        ch.link(nc.vector.scalar_tensor_tensor(out=hot, in0=lg, scalar=topv[:, u, k:k + 1],
                                                               in1=desc[:, :], op0=ALU.is_equal, op1=ALU.mult))
                        ch.link(nc.vector.reduce_max(small[:, 0:1], hot, AX.X))
                        ch.link(nc.vector.tensor_scalar(hot4[:, k, :], desc[:, :], small[:, 0:1], None, ALU.is_equal))
                        if k < TOPK - 1:
                            ch.link(nc.vector.scalar_tensor_tensor(out=lg, in0=hot4[:, k, :], scalar=-3e38, in1=lg,
                                                                   op0=ALU.mult, op1=ALU.add))
                    ch.link(nc.vector.tensor_tensor(hots, hot4[:, 0, :], hot4[:, 1, :], ALU.add))
                    ch.link(nc.vector.tensor_tensor(prod, hot4[:, 2, :], hot4[:, 3, :], ALU.add))
                    nc.vector.tensor_tensor(hots, hots, prod, ALU.add).then_inc(s_hot, 1)
                    nc.vector.tensor_scalar(gates[:, u, :], topv[:, u, :], topv[:, u, 0:1], None, ALU.subtract
                                            ).then_inc(s_ex2, 1)
                    dve.wait_ge(s_g4, u + 1)
                    ch.link(nc.vector.reciprocal(gsum[:, u:u + 1], gsum[:, u:u + 1]))
                    ch.link(nc.vector.tensor_scalar(gates[:, u, :], gates[:, u, :], gsum[:, u:u + 1], None, ALU.mult))
                    ch.link(nc.vector.tensor_scalar(G[:, u, :], hot4[:, 0, :], gates[:, u, 0:1], None, ALU.mult))
                    for k in range(1, TOPK):
                        ch.link(nc.vector.scalar_tensor_tensor(out=G[:, u, :], in0=hot4[:, k, :],
                                                               scalar=gates[:, u, k:k + 1], in1=G[:, u, :],
                                                               op0=ALU.mult, op1=ALU.add))
                    dve.wait_ge(s_rank, u + 1)
                    ch.link(nc.vector.tensor_tensor(rk, ps[:, 7, 0:E], seen[:, :], ALU.add))
                    nc.vector.tensor_tensor(seen[:, :], ps[:, 7, E:2 * E], seen[:, :], ALU.add).then_inc(s_rku, 1)
                    ch.link(nc.vector.tensor_tensor(rk, rk, eoff[:, :], ALU.add))
                    for k in range(TOPK):
                        ch.link(nc.vector.tensor_tensor(prod, hot4[:, k, :], rk, ALU.mult))
                        ch.link(nc.vector.reduce_sum(slot_f[:, k:k + 1], prod, AX.X))
                        nc.vector.tensor_copy(entry[:, u, k, 0:1], itok[:, u:u + 1])
                        nc.vector.tensor_scalar(entry[:, u, k, 1:2], itok[:, u:u + 1], float(k * T), None, ALU.add)
                    nc.vector.tensor_copy(slot_i[:, u, :], slot_f[:, :]).then_inc(s_slot, 1)
            ch.link(nc.vector.reduce_max(small[:, 1:2], seen[:, :], AX.X))
            nc.vector.tensor_scalar(flags[:, :], iexp[:, 0:8], float(C), small[:, 1:2], ALU.mult, ALU.is_lt
                                    ).then_inc(s_flag, 1)
            dve.wait_ge(s_mi, 4 * 16)
            ch.link(nc.vector.tensor_scalar(gub1, gub, 1.0, None, ALU.add))

            def expert_dve(r):
                with dve.Fori(0, E) as e:
                    n = r * E + e
                    for f in range(KT):
                        b = f % 2
                        dve.wait_ge(s_gu, 8 * n + f + 1)
                        nc.vector.tensor_scalar(gt[b], ps[:, b, 0:C], gub[:, bass.ds(e * 16 + 2 * f, 1)], LIMIT,
                                                ALU.add, ALU.min).then_inc(s_g1, 1)
                        nc.vector.tensor_scalar(lt[b], ps[:, b, C:2 * C], gub1[:, bass.ds(e * 16 + 2 * f + 1, 1)],
                                                LIMIT + 1, ALU.add, ALU.min).then_inc(s_gd, 1)
                        dve.wait_ge(s_gd, 8 * n + f + 1)
                        dve.wait_ge(s_gs, 8 * n + f + 1)
                        nc.vector.scalar_tensor_tensor(out=lt[b], in0=lt[b], scalar=1 - LIMIT, in1=sgm[b],
                                                       op0=ALU.max, op1=ALU.mult).then_inc(s_l1, 1)
                        dve.wait_ge(s_l1, 8 * n + f + 1)
                        nc.vector.tensor_tensor(actT[:, f, :], lt[b], gt[b], ALU.mult).then_inc(s_act, 1)
                    for q in range(4):
                        dve.wait_ge(s_yt, 4 * n + q + 1)
                        if q == 0:
                            dve.wait_ge(s_scr, n + 1)
                        hh = slice(q % 2 * HALF, (q % 2 + 1) * HALF)
                        if q < 2:
                            nc.vector.tensor_copy(Yt[:, hh], ps[:, 6 + q, :]).then_inc(s_ye, 1)
                        else:
                            nc.vector.tensor_copy(Y2[0:C2, hh], ps[0:C2, 2 + q, :]).then_inc(s_ye, 1)

            rounds(dve, expert_dve)

            dve.wait_ge(s_fi, 32)
            for t in range(TT):
                dve.wait_ge(s_bp, 2 * t + 2)
                b = 2 + 2 * (t % 2)
                nc.vector.tensor_tensor(h_sb[:, t, 0:HALF], ps[:, b, :], h_sb[:, t, 0:HALF], ALU.add)
                last = nc.vector.tensor_tensor(h_sb[:, t, HALF:D], ps[:, b + 1, :], h_sb[:, t, HALF:D], ALU.add)
                dve.wait_ge(s_yl[t % 2], 16 * (t // 2 + 1))
                for k in range(TOPK):
                    last.then_inc(s_fs, 1)
                    dve.wait_ge(s_fs, TOPK * t + k + 1)
                    last = nc.vector.scalar_tensor_tensor(out=h_sb[:, t, :], in0=ypair[t % 2][:, k, :],
                                                          scalar=gates[:, t, k:k + 1], in1=h_sb[:, t, :],
                                                          op0=ALU.mult, op1=ALU.add)
                last.then_inc(s_hf, 1)
                dve.wait_ge(s_sq2, TT + t + 1)
                nc.vector.tensor_scalar(stat3[:, 1, t:t + 1], stat3[:, 0, t:t + 1], 1.0 / D, RMS_EPS,
                                        ALU.mult, ALU.add).then_inc(s_ms2, 1)
                dve.wait_ge(s_rt2, TT + t + 1)
                ch.link(nc.vector.reciprocal(stat3[:, 2, t:t + 1], stat3[:, 1, t:t + 1]))
                if t >= 2:
                    dve.wait_ge(s_out[t % 2], 16 * (t // 2))
                nc.vector.scalar_tensor_tensor(out=fin[t % 2], in0=h_sb[:, t, :], scalar=stat3[:, 2, t:t + 1],
                                               in1=nw3, op0=ALU.mult, op1=ALU.mult).then_inc(s_o, 1)

        @block.tensor
        def _(pe):
            pe.wait_ge(s_par, 4 * 16)
            for t in range(TT):
                pe.wait_ge(s_xn, t + 1)
                for g in range(2):
                    if t >= 2:
                        pe.wait_ge((s_te, s_tv)[g], t - 1)
                    for k in range(4):
                        kt = 4 * g + k
                        last = nc.tensor.transpose(ps[:, 2 * (t % 2) + g, k * P:(k + 1) * P],
                                                   xs[:, t, kt * P:(kt + 1) * P], ident)
                    last.then_inc(s_tr, 1)
            pe.wait_ge(s_te, TT)
            pe.wait_ge(s_tv, TT)

            def project(slot, bank, h):
                for kt in range(KT):
                    last = nc.tensor.matmul(ps[:, bank + h, :], win[:, slot, kt * P:(kt + 1) * P],
                                            xnT[:, kt, h * HALF:(h + 1) * HALF], start=kt == 0, stop=kt == KT - 1)
                return last

            def tile(n, between=None):
                pe.wait_ge(s_w[n % 3], 16 * (n // 3 + 1))
                for h in range(2):
                    if n >= 3:
                        pe.wait_ge(s_pc, 2 * (n - 3) + h + 1)
                    project(n % 3, ring_pair(n), h).then_inc(s_pj, 1)
                    if h == 0 and between is not None:
                        between()

            def bonus(i):
                def go():
                    pe.wait_ge(s_rk, i + 1)
                    for h in range(2):
                        nc.tensor.matmul(ps[:, 6 + h, :], ones2, W8[:, h * HALF:(h + 1) * HALF],
                                         start=True, stop=True).then_inc(s_pm, 1)
                return go

            tile(0)
            tile(1)
            for i in range(RT):
                n = 2 + 3 * i
                tile(n, bonus(i - 1) if i else None)
                pe.wait_ge(s_lo, 1)
                if i:
                    pe.wait_ge(s_bu, i)
                for h in range(2):
                    nc.tensor.matmul(ps[:, 6 + h, :], lora[0:LORA, i * P:(i + 1) * P],
                                     tdwa[0:LORA, h * HALF:(h + 1) * HALF], start=True, stop=True).then_inc(s_pm, 1)
                tile(n + 1)
                for h in range(2):
                    pe.wait_ge(s_sg, 4 * i + h + 1)
                    nc.tensor.matmul(ps[:, 6 + h, :], lora[LORA:P, i * P:(i + 1) * P],
                                     tdwa[LORA:P, h * HALF:(h + 1) * HALF], start=True, stop=True).then_inc(s_pm, 1)
                tile(n + 2)
                pe.wait_ge(s_sk, i + 1)
                for h in range(2):
                    pe.wait_ge(s_sg, 4 * i + 2 + h + 1)
                    nc.tensor.matmul(ps[:, 6 + h, :], ones2, W8[:, h * HALF:(h + 1) * HALF],
                                     start=True, stop=True).then_inc(s_pm, 1)
            with pe.Fori(0, RT) as i:
                for j in range(3):
                    pe.wait_ge(s_wcv[j], 16 * i + 16)
                    for h in range(2):
                        if j == 0:
                            pe.wait_ge(s_ccp, 2 * i + 1)
                            pe.wait_ge(s_pc, 2 * NR)
                        elif j == 1:
                            pe.wait_ge(s_u, 2 * i + 1)
                        else:
                            pe.wait_ge(s_cd, 2 * i + 1)
                        project((NR + j) % 3, ring_pair(NR + j), h).then_inc(s_pcv, 1)
            bonus(RT - 1)()

            heads = [(r, h) for r in range(RT) for h in range(2)]
            own = lambda h: slice(N * h, N * h + N)
            other = lambda h: slice(N * (1 - h), N * (1 - h) + N)
            pe.wait_ge(s_zv, 1)
            pe.wait_ge(s_bu, RT)
            with pe.Fori(0, NCH // 2) as it:
                for s in range(2):
                    b = 4 * s
                    pe.wait_ge(s_st[s], 48 * it + 48)
                    pe.wait_ge(s_yc[s], it + 1)
                    pe.wait_ge(s_s[s], it + 1)
                    for r, h in heads:
                        o = own(h)
                        last = nc.tensor.matmul(ps[:, b + h, r * P:(r + 1) * P],
                                                BKc[s][o, r, :, :].rearrange("p k t -> p (k t)"),
                                                ARc[s][o, r, :, :].rearrange("p k t -> p (k t)"), start=True, stop=True)
                    last.then_inc(s_g, 1)
                    for r, h in heads:
                        o = own(h)
                        last = nc.tensor.matmul(ps[other(h), b + 3, r * L:(r + 1) * L], Vc[s][o, r, :],
                                                cst[o, K_ID2:K_ID2 + L], start=True, stop=True)
                    last.then_inc(s_v, 1)
                    for r, h in heads:
                        o = own(h)
                        nc.tensor.matmul(ps[o, b + 2, r * L:(r + 1) * L], ARc[s][o, r, 0, :],
                                         BKc[s][o, r, h, :], start=True, stop=True)
                        last = nc.tensor.matmul(ps[o, b + 2, (RT + r) * L:(RT + r + 1) * L], ARc[s][o, r, 0, :],
                                                cst[o, K_ID2:K_ID2 + L], start=True, stop=True)
                    last.then_inc(s_m, 1)
                for s in range(2):
                    b = 4 * s
                    pe.wait_ge(s_bs, 2 * it + s + 1)
                    pe.wait_ge(s_ac, 2 * it + s + 1)
                    pe.sem_inc(s_pe_apart, 1)
                    for n, (r, h) in enumerate(heads):
                        o = own(h)
                        last = nc.tensor.transpose(ps[:, b + 3 - h, r * L:(r + 1) * L],
                                                   BKs[s][o, r, :, :].rearrange("p k t -> p (k t)"),
                                                   ident[o, N * h:N * h + N])
                    last.then_inc(s_bt, 1)
                for l in range(len(LEVELS)):
                    for s in range(2):
                        b = 4 * s
                        pe.wait_ge(s_t[s], 5 * it + l + 1)
                        if l == 0:
                            pe.wait_ge(s_mt, 2 * it + s + 1)
                            pe.wait_ge(s_gm[s], 2 * it + 2)
                        for r in range(RT):
                            last = nc.tensor.matmul(ps[:, b, r * L:(r + 1) * L], MTb[s][:, r].rearrange("p k t -> p (k t)"),
                                                    Tst[s][:, r, :], start=True, stop=True)
                        last.then_inc(s_pe_e[s], 1)
                    if l == 0:
                        for s in range(2):
                            b = 4 * s
                            pe.wait_ge(s_bc[s], 2 * it + 2)
                            pe.sem_inc(s_pe_apart, 1)
                            for n, (r, h) in enumerate(heads):
                                last = nc.tensor.matmul(ps[own(h), b + 3, r * L:(r + 1) * L], Gm[s][other(h), n, 0:L],
                                                        SAV[s][other(h), n, :], start=True, stop=True)
                            last.then_inc(s_nv, 1)
                    for s in range(2):
                        b = 4 * s
                        if l == 0:
                            pe.wait_ge(s_tt0[s], 2 * it + 2)
                        else:
                            pe.wait_ge(s_tt[s], 5 * it + l)
                        if l < 4:
                            pe.wait_ge(s_e[s], 10 * it + 2 * l + 1)
                            for r in range(RT):
                                last = nc.tensor.matmul(ps[:, b + 2, r * L:(r + 1) * L],
                                                        TTb[s][:, r].rearrange("p k t -> p (k t)"),
                                                        Est[s][:, r, :], start=True, stop=True)
                            last.then_inc(s_pe_f[s], 1)
                        pe.wait_ge(s_e[s], 10 * it + 2 * l + 2)
                        for r in range(RT):
                            last = nc.tensor.matmul(ps[:, b + 1, r * P:(r + 1) * P],
                                                    Ebd[s][:, r].rearrange("p k t -> p (k t)"),
                                                    TTb[s][:, r].rearrange("p k t -> p (k t)"), start=True, stop=True)
                        last.then_inc(s_pe_ft[s], 1)
                for s in range(2):
                    b = 4 * s
                    pe.wait_ge(s_tt[s], 5 * it + 5)
                    pe.wait_ge(s_nvc, 2 * it + s + 1)
                    pe.sem_inc(s_pe_apart, 1)
                    for r, h in heads:
                        last = nc.tensor.matmul(ps[own(h), b + 3, r * L:(r + 1) * L], MAt[s][own(h), 1, r, :],
                                                TTb[s][own(h), r, h, :], start=True, stop=True)
                    last.then_inc(s_ut, 1)
                for s in range(2):
                    b = 4 * s
                    pe.wait_ge(s_nvc, 2 * it + s + 1)
                    pe.wait_ge(s_utc, 2 * it + s + 1)
                    pe.wait_ge(s_bc[s], 2 * it + 2)
                    if s == 0:
                        pe.wait_ge(s_s[1], it + 1)
                    else:
                        pe.wait_ge(s_s[0], it + 2)
                    for r in range(RT):
                        nc.tensor.matmul(ps[:, b + 2, r * L:(r + 1) * L], TTb[s][:, r].rearrange("p k t -> p (k t)"),
                                         NVs[s][:, r, :], start=True, stop=False)
                        last = nc.tensor.matmul(ps[:, b + 2, r * L:(r + 1) * L],
                                                UTb[s][:, r].rearrange("p k t -> p (k t)"), St[s][:, r, :],
                                                start=False, stop=True)
                    last.then_inc(s_sa, 1)
                    pe.wait_ge(s_sac, 2 * it + s + 1)
                    for n, (r, h) in enumerate(heads):
                        last = nc.tensor.matmul(ps[own(h), b + 3, r * L:(r + 1) * L], BKt[s][:, n, :],
                                                SAV[s][:, n, :], start=True, stop=True)
                    last.then_inc(s_sn, 1)
                    for n, (r, h) in enumerate(heads):
                        nc.tensor.matmul(ps[own(h), b + 1, r * L:(r + 1) * L], SAV[s][:, n, :], Gm[s][:, n, L:2 * L],
                                         start=True, stop=False)
                        last = nc.tensor.matmul(ps[own(h), b + 1, r * L:(r + 1) * L], St[s][own(h), r, :],
                                                ARc[s][own(h), r, 1, :], start=False, stop=True)
                    last.then_inc(s_y[s], 1)

            for k in range(2):
                pe.wait_ge(s_yc[k], NCH // 2 + 1)
                pe.wait_ge(s_s[k], NCH // 2 + 1)
            pe.wait_ge(s_pi, 16 * (RT + 1))
            for i in range(RT):
                for h in range(2):
                    if i:
                        pe.wait_ge(s_yc2, 2 * i)
                    nc.tensor.matmul(ps[:, h, :], ones2, YF[:, i, h * HALF:(h + 1) * HALF],
                                     start=True, stop=True).then_inc(s_mp, 1)
                for h in range(2):
                    if i:
                        pe.wait_ge(s_mix, i)
                    nc.tensor.matmul(ps[:, 4 + h, :], wgate[:, i * P:(i + 1) * P], sdg[:, h * HALF:(h + 1) * HALF],
                                     start=True, stop=True).then_inc(s_gp, 1)
                pe.wait_ge(s_ysq, i + 1)
                for h in range(2):
                    nc.tensor.matmul(ps[:, 2 + h, :], ones2, gn_sq[i % 2][:, h * HALF:(h + 1) * HALF],
                                     start=True, stop=True).then_inc(s_vp, 1)

            pe.wait_ge(s_wo, 16 * (RT + 2))
            pe.wait_ge(s_mi, 3 * 16)
            pe.wait_ge(s_mix, RT)
            for t in range(TT + 2):
                if t < TT:
                    for h in range(2):
                        if t >= 2:
                            pe.wait_ge(s_h, t - 1)
                        for k in range(2 * RT):
                            last = nc.tensor.matmul(ps[:, 2 * (t % 2) + h, :], mixT[:, k, t * P:(t + 1) * P],
                                                    wo[:, k, h * HALF:(h + 1) * HALF], start=k == 0, stop=k == 2 * RT - 1)
                        last.then_inc(s_op, 1)
                if t >= 2:
                    u = t - 2
                    pe.wait_ge(s_hot, u + 1)
                    if u:
                        pe.wait_ge(s_rku, u)
                    nc.tensor.matmul(ps[:, 7, 0:E], tri, hots, start=True, stop=True)
                    nc.tensor.matmul(ps[:, 7, E:2 * E], ones, hots, start=True, stop=True).then_inc(s_rank, 1)
                if 1 <= t <= TT:
                    u = t - 1
                    pe.wait_ge(s_xn2, u + 1)
                    for g in range(2):
                        if u:
                            pe.wait_ge(s_t2c, 2 * u + g - 1)
                        for k in range(4):
                            kt = 4 * g + k
                            last = nc.tensor.transpose(ps[:, 4 + g, k * P:(k + 1) * P], xn2[u % 2][:, kt * P:(kt + 1) * P],
                                                       ident)
                        last.then_inc(s_t2, 1)
                    pe.wait_ge(s_t2c, 2 * u + 2)
                    if u:
                        pe.wait_ge(s_lgu, u)
                    for kt in range(KT):
                        last = nc.tensor.matmul(ps[:, 6, 0:E], xn2T[u % 2][:, kt, :], rw[:, kt, :],
                                                start=kt == 0, stop=kt == KT - 1)
                    last.then_inc(s_lg, 1)
            pe.wait_ge(s_rku, TT)

            def transpose_tokens(m):
                pe.wait_ge(s_gx, 32 * m + 32)
                for q in range(4):
                    if q >= 2:
                        pe.wait_ge(s_xe, 4 * m + q - 1)
                    for k in range(2):
                        kt = 2 * q + k
                        nc.tensor.transpose(ps[:, 4 + q % 2, k * C:k * C + P], xg[:, kt * P:(kt + 1) * P], ident)
                        last = nc.tensor.transpose(ps[:, 4 + q % 2, k * C + P:(k + 1) * C],
                                                   xg2[0:C2, kt * P:(kt + 1) * P], ident[0:C2, 0:C2])
                    last.then_inc(s_xt, 1)

            def expert_pe(r):
                pe.wait_ge(s_ye, 4 * r * E + 1)
                transpose_tokens(r * (E + 1))
                with pe.Fori(0, E) as e:
                    n, m = r * E + e, r * (E + 1) + e + 1
                    pe.wait_ge(s_xe, 4 * m)
                    for f in range(KT):
                        u = f // 2
                        if f % 2 == 0:
                            pe.wait_ge(s_wt[u], 16 * n + 16)
                        if f >= 2:
                            pe.wait_ge(s_gd, 8 * n + f - 1)
                        for k in range(2):
                            for kt in range(KT):
                                o = f % 2 * 2 * P + k
                                last = nc.tensor.matmul(ps[:, f % 2, k * C:(k + 1) * C], wslot[u][:, kt, o:o + 2 * P - 1:2],
                                                        xT[:, kt, :], start=kt == 0, stop=kt == KT - 1)
                        last.then_inc(s_gu, 1)
                    pe.wait_ge(s_ye, 4 * n + 1)
                    transpose_tokens(m)
                    for d in range(KT):
                        u = 4 + d // 4
                        if d == 0:
                            pe.wait_ge(s_act, 8 * n + 8)
                        if d % 4 == 0:
                            pe.wait_ge(s_wt[u], 16 * n + 16)
                        if d >= 2:
                            pe.wait_ge(s_dd, 8 * n + d - 1)
                        for ft in range(KT):
                            last = nc.tensor.matmul(ps[:, 2 + d % 2, 0:C], wslot[u][:, ft, d % 4 * P:(d % 4 + 1) * P],
                                                    actT[:, ft, :], start=ft == 0, stop=ft == KT - 1)
                        last.then_inc(s_dn, 1)
                    for q in range(4):
                        pe.wait_ge(s_dd, 8 * n + 4 + 4 * (q % 2))
                        for k in range(4):
                            d = q % 2 * 4 + k
                            if q < 2:
                                last = nc.tensor.transpose(ps[:, 6 + q, k * P:(k + 1) * P], yT[:, d, 0:P], ident)
                            else:
                                last = nc.tensor.transpose(ps[0:C2, 2 + q, k * P:(k + 1) * P], yT[:, d, P:C], ident)
                        last.then_inc(s_yt, 1)

            rounds(pe, expert_pe)

            pe.wait_ge(s_md, 1)
            for t in range(TT):
                last = nc.tensor.transpose(ps[0:E, t // 4, t % 4 * P:(t % 4 + 1) * P], G[:, t, :], ident)
            last.then_inc(s_gT, 1)
            pe.wait_ge(s_gTc, 1)
            pe.wait_ge(s_fi, 32)
            for t in range(TT):
                for h in range(2):
                    if t >= 2:
                        pe.wait_ge(s_hf, t - 1)
                    nc.tensor.matmul(ps[:, 2 + 2 * (t % 2) + h, :], GT[0:E, t, :], dnb[0:E, h * HALF:(h + 1) * HALF],
                                     start=True, stop=True).then_inc(s_bp, 1)


IN_TILES = ([3072, 3200] + [1536 + k * 512 + i * P for i in range(4) for k in range(3)]
            + [[512, 1024, 0][k] + i * P for i in range(4) for k in range(3)])


def kernel(**a):
    import concourse.bacc as _bacc
    from concourse.bass_utils import run_bass_kernel_spmd as _run

    a = {k: np.asarray(v) for k, v in a.items()}
    nc = _bacc.Bacc("TRN2", target_bir_lowering=False, num_devices=1)

    def cols(v):
        return v.reshape(-1, P).T

    conv = a["conv_w"][0].reshape(3, RT, P).transpose(2, 1, 0).reshape(P, 12)
    prm = np.ascontiguousarray(np.concatenate(
        [cols(a["mu_shift"][0]), cols(a["w0"][0]), cols(a["a0"][0]), cols(a["k_k"][0]), cols(a["k_a"][0]),
         cols(a["r_k"][0].reshape(-1)), cols(a["ln_x_w"][0]), cols(a["ln_x_b"][0]), conv], axis=1))
    w_in = a["w_in"][0]
    w_in_t = np.stack([w_in[:, o:o + P].reshape(KT, P, P).transpose(1, 0, 2).reshape(P, KT * P) for o in IN_TILES])
    rep = lambda v: np.ascontiguousarray(np.broadcast_to(v, (P, v.shape[-1])))
    arrays = {
        "x": a["x"][0],
        "w_in_t": w_in_t,
        "prm": prm,
        "lora": np.concatenate([a["w_decay_up"][0], a["w_iclr_up"][0]]),
        "wgate": a["w_gate_up"][0],
        "normw": np.stack([rep(a["norm_mix_w"][0]), rep(a["norm_ffn_w"][0]), rep(a["norm_final_w"])]),
        "w_out": a["w_out"][0],
        "router_w": a["router_w"][0],
        "router_b": rep(a["router_b"][0]),
        "gub": np.ascontiguousarray(a["gu_b"][0].reshape(E, KT, P, 2).transpose(2, 0, 1, 3).reshape(P, E * 2 * KT)),
        "gu_w": a["gu_w"][0],
        "dn_w": a["dn_w"][0],
        "dn_b": a["dn_b"][0],
        "consts": constants(),
        "list0": np.tile(np.array([[0, SKIP]], np.int32), ((E + 1) * LIST, 1)),
    }
    arrays = {k: np.ascontiguousarray(v) for k, v in arrays.items()}
    args = [nc.dram_tensor(n, v.shape, mybir.dt.from_np(v.dtype), kind="ExternalInput").ap()
            for n, v in arrays.items()]
    out = nc.dram_tensor("out", (T, D), FP, kind="ExternalOutput").ap()
    scratch = [("conv_s", (RT, P, T), FP), ("bonus_s", (RT, P, T), FP), ("xn_s", (T, D), FP),
               ("pair_s", (PAIRS, D), FP), ("list_s", ((E + 1) * LIST, 2), I32), ("flag_s", (1, 8), I32)]
    args.append(out)
    args += [nc.dram_tensor(n, s, d, kind="Internal").ap() for n, s, d in scratch]
    build(nc, *args)
    r = _run(nc, [arrays], core_ids=[0])
    return r.results[0]["out"].reshape(1, T, D)
```

```python
import concourse.bass as bass
from concourse import mybir
from contextlib import ExitStack
import math
import numpy as np

FP = mybir.dt.float32
I32 = mybir.dt.int32
ALU = mybir.AluOpType
ACT = mybir.ActivationFunctionType
AX = mybir.AxisListType

P = 128
T = 1024
D = 1024
KT = D // P
TT = T // P
HALF = 512
CONV = 512
RW = 512
RT = RW // P
N = 64
L = 64
NCH = T // L
LORA = 64
E = 32
TOPK = 4
F = 1024
C = 256
SIZES = [112, 120, 128, 136, 144, 160, 192, C]
ROUNDS = -(-T // C)
LIST = ROUNDS * C
PAIRS = T * TOPK
SKIP = 1 << 20
RMS_EPS = 1e-5
GN_EPS = 64e-5
KAPPA = math.exp(-0.5)
LIMIT = 7.0
ALPHA = 1.702
LEVELS = [2, 4, 8, 16, 32]

MU, W0, A0, KKW, KAW, RKW, LNW, LNB, CVW = 0, 14, 18, 22, 26, 30, 34, 38, 42
NPRM = 54

K_ID, K_ONES2, K_MG, K_ID2, K_M1, K_ME, K_BD, K_MTB = 0, 128, 256, 384, 448, 512, 832, 960
K_MIX = 960 + 128 * 6
K_TRI, K_ALL, K_EXP, K_TOK = K_MIX, K_MIX + 128, K_MIX + 256, K_MIX + 288
NCONST = K_MIX + 288 + TT


def constants():
    c = np.zeros((P, NCONST), np.float32)
    p = np.arange(P)[:, None]
    q = np.arange(P)[None, :]
    t = np.arange(L)[None, :]
    pl = p % L
    c[:, K_ID:K_ID + P] = p == q
    c[:, K_ONES2:K_ONES2 + P] = p // N == q // N
    c[:, K_MG:K_MG + L] = pl < t
    c[:, K_MG + L:K_MG + 2 * L] = pl <= t
    c[:, K_ID2:K_ID2 + L] = pl == t
    same = p // L == q // L

    def off(b, row, col):
        return (row // b % 2 == 1) & (col // b == row // b - 1)

    c[:, K_M1:K_M1 + L] = off(1, pl, t)
    for n, b in enumerate(LEVELS):
        c[:, K_ME + n * L:K_ME + (n + 1) * L] = off(b, pl, t)
        c[:, K_MTB + n * P:K_MTB + (n + 1) * P] = same & off(b, pl, q % L)
    c[:, K_BD:K_BD + P] = same & off(1, q % L, pl)
    c[:, K_MTB + 5 * P:K_MTB + 6 * P] = same
    c[:, K_TRI:K_TRI + P] = p < q
    c[:, K_ALL:K_ALL + P] = 1.0
    c[:, K_EXP:K_EXP + E] = np.arange(E)[None, :]
    c[:, K_TOK:K_TOK + TT] = np.arange(TT)[None, :] * P + p
    return c


class Chain:

    def __init__(self, eng, sem, base=0):
        self.eng, self.sem, self.base, self.n = eng, sem, base, 0

    def link(self, ins):
        self.n += 1
        ins.then_inc(self.sem, 1)
        self.eng.wait_ge(self.sem, self.base + self.n)


def build(nc, x, w_in_t, prm_d, lora_d, wgate_d, normw_d, w_out, router_w, router_b, gub_d, gu_w, dn_w,
          dn_b, consts_d, list0_d, out, conv_d, bonus_d, xn_d, pair_d, list_d, flag_d, stop=99):
    ctx = ExitStack()
    with ctx:
        def sem(name):
            return ctx.enter_context(nc.semaphore(name))

        def sb(name, shape, dt=FP):
            return ctx.enter_context(nc.sbuf_tensor(name, shape, dt))

        arena = sb("arena", [P, 196 * 256])

        def at(kb, *shape):
            n = math.prod(shape)
            o = int(kb * 256)
            v = arena[:, o:o + n]
            if len(shape) == 2:
                v = v.rearrange("p (a b) -> p a b", b=shape[1])
            elif len(shape) == 3:
                v = v.rearrange("p (a b c) -> p a b c", b=shape[1], c=shape[2])
            elif len(shape) == 4:
                v = v.rearrange("p (a b c d) -> p a b c d", b=shape[1], c=shape[2], d=shape[3])
            return v

        ps = ctx.enter_context(nc.psum_tensor("ps", [P, 8, HALF], FP))
        cst = sb("cst", [P, K_MIX])
        prm = sb("prm_sb", [P, NPRM])
        omka = sb("omka", [P, RT])
        stat = sb("stat", [P, 3, TT])
        cL = sb("cL", [P, RT, NCH])
        ident = cst[:, K_ID:K_ID + P]
        ones2 = cst[:, K_ONES2:K_ONES2 + P]

        xs = at(0, TT, D)
        sqj = at(32, D)
        nw = at(36, D)
        AR = at(0, RT, NCH, 2, L)
        BK = at(32, RT, NCH, 2, L)
        V = at(64, RT, T)
        conv_st = at(80, 2, T)
        bonus_st = at(88, 2, T)
        xnT = at(96, KT, T)
        win = at(128, 3, KT * P)
        praw = at(140, 2, 1028)
        q_r, q_k, W1, W2, W3, W4, W6, W7, W8 = (at(149 + 4 * n, T) for n in range(9))
        u_cv = at(140, 1028)
        ccs = at(145, T)
        t_cv = at(149, T)
        tdwa = at(185, T)
        lora = at(189, RW)
        sdg = at(192, T)

        YF = at(96, RT, T)
        CB = 28
        ARc, BKc, BKs, MTb, TTb, Ebd, UTb = (
            [at(128 + CB * s + o, RT, 2, L) for s in range(2)] for o in (0, 2, 4, 6, 8, 10, 12))
        Gm, = ([at(128 + CB * s + o, 2 * RT, 2 * L) for s in range(2)] for o in (14,))
        BKt, SAV = ([at(128 + CB * s + o, 2 * RT, L) for s in range(2)] for o in (18, 20))
        Vc, Tst, Est, NVs = ([at(128 + CB * s + o, RT, L) for s in range(2)] for o in (22, 23, 24, 25))
        MAt = [at(128 + CB * s + 26, 2, RT, L) for s in range(2)]
        St = [at(184 + s, RT, L) for s in range(2)]
        Sc = at(186, RT, L)

        mixT = at(128, 2 * RT, T)
        bonus_in = at(112, RT, T)
        gn_yc, gn_sq, gn_sd = ([at(64 + 12 * s + o, T) for s in range(2)] for o in (0, 4, 8))
        wgate = at(88, RW)
        wo = at(160, KT, D)
        h_sb = at(96, TT, D)
        xres = [at(64 + 4 * s, D) for s in range(2)]
        sqj2 = at(72, D)
        xn2 = [at(76 + 4 * s, D) for s in range(2)]
        xn2T = [at(84 + 4 * s, KT, P) for s in range(2)]
        nw2 = at(92, D)
        rw = at(192, KT, E)
        lg, hot, prod, rk = (at(193 + n * 0.125, E) for n in range(4))
        hots = [at(193.5 + s * 0.125, E) for s in range(2)]
        hot4 = [at(194 + s * 0.5, TOPK, E) for s in range(2)]
        rb = at(193.875, E)
        G = at(195, TT, E)
        cst2 = sb("cst2", [P, NCONST - K_MIX])
        tri, ones, iexp, itok = (cst2[:, a - K_MIX:b - K_MIX] for a, b in (
            (K_TRI, K_ALL), (K_ALL, K_EXP), (K_EXP, K_TOK), (K_TOK, NCONST)))
        desc = sb("desc", [P, E])
        eoff = sb("eoff", [P, E])
        seen = sb("seen", [P, E])
        topv = sb("topv", [P, TT, TOPK])
        gates = sb("gates", [P, TT, TOPK])
        small = sb("small", [P, 8])
        gneps = sb("gneps", [P, 1])
        gsum = sb("gsum", [P, TT])
        slot_f = sb("slot_f", [P, TOPK])
        slot_i = sb("slot_i", [P, TT, TOPK], I32)
        entry = sb("entry", [P, TT, TOPK, 2], I32)
        flags = sb("flags", [P, 8], I32)
        size_f = at(194, ROUNDS, E)
        left = at(193.75, E)
        size_i = sb("size_i", [P, ROUNDS * E], I32)
        stat2 = sb("stat2", [P, 3, TT])
        stat3 = sb("stat3", [P, 3, TT])
        wslot = [at(16 * u, KT, HALF) for u in range(6)]
        xg = at(128, D)
        xg2 = at(132, D)
        xT = at(136, KT, C)
        actT = at(144, KT, C)
        yT = at(152, KT, C)
        Yt = at(160, D)
        Y2 = at(164, D)
        gub = at(168, E * 2 * KT)
        gub1 = at(170, E * 2 * KT)
        gt, lt, sgm = ([at(172 + 2 * k + s, C) for s in range(2)] for k in range(3))
        idx_g = sb("idx_g", [P, 2], I32)
        idx_g2 = sb("idx_g2", [P, 2], I32)
        idx_s = sb("idx_s", [P, 2], I32)
        idx_s2 = sb("idx_s2", [P, 2], I32)
        ypair = [at(base, TOPK, D) for base in (0, 16, 64)]
        dgate = at(128, TT, P)
        dnb = at(40, D)
        GT = at(44, TT, P)
        nw3 = at(48, D)
        sqj3 = at(52, D)
        fin = [at(56 + 4 * s, D) for s in range(2)]

        s_x = [sem(f"x_in{t}") for t in range(2)]
        s_par = sem("params_in")
        s_sq = sem("squares")
        s_ms = sem("mean_square")
        s_rt = sem("root")
        s_xn = sem("x_normalised")
        s_tr = sem("x_transposed")
        s_te = sem("xT_evacuated_act")
        s_tv = sem("xT_evacuated_dve")
        s_w = [sem(f"w_in{k}") for k in range(3)]
        s_pj = sem("projected")
        s_pc = sem("praw_copied")
        s_pu = sem("praw_used")
        s_lo = sem("lora_acts")
        s_pm = sem("prep_products")
        s_sg = sem("sigmoids")
        s_cu = sem("cumulated")
        s_ex = sem("exps")
        s_kk = sem("kk_ready")
        s_sk = sem("kk_squared")
        s_nr = sem("norms")
        s_td = sem("tile_done")
        s_rk = sem("rk_ready")
        s_bu = sem("bonus_made")
        s_bo = [sem(f"bonus_out{k}") for k in range(2)]
        s_dv = sem("dve_step")
        s_ccp = sem("cc_copied")
        s_u = sem("u_made")
        s_cd = sem("conv_done")
        s_cvo = sem("conv_out")
        s_cds = sem("conv_step")
        s_pz = sem("pads_zero")
        s_pcv = sem("conv_projected")
        s_wcv = [sem(f"w_conv{k}") for k in range(3)]

        two = lambda name: [sem(f"{name}{s}") for s in range(2)]
        s_z = sem("chunk_buffers_zero")
        s_zv = sem("state_zero")
        s_st = two("chunk_staged")
        s_bs = sem("BK_scaled")
        s_g, s_m, s_v, s_bt = sem("scores"), sem("M_and_At"), sem("Vt"), sem("BKt")
        s_gm, s_mt, s_tt0 = two("scores_masked"), sem("MT_copied"), two("TT_first")
        s_ac, s_bc = sem("At_copied"), two("BKt_copied")
        s_pe_e, s_pe_f, s_pe_ft = two("E"), two("F"), two("FT")
        s_e, s_t, s_tt = two("E_masked"), two("T_updated"), two("TT_updated")
        s_nv, s_ut, s_nvc, s_utc = sem("NV"), sem("UT"), sem("NV_copied"), sem("UT_copied")
        s_sa, s_sac, s_sn, s_s = sem("SA"), sem("SA_copied"), sem("state_product"), two("state")
        s_y, s_yc = two("Y"), two("Y_copied")
        s_cst = sem("chunk_step")
        s_xz, s_sz = sem("xg_zero"), sem("sizes_ready")
        s_cvr, s_scr = sem("conv_stage_free"), sem("expert_rows_free")
        s_pe_apart, s_pool_apart = sem("pe_apart"), sem("pool_apart")
        s_pi = sem("post_inputs")
        s_wo = sem("w_out_in")
        s_mp, s_vp, s_gp = sem("mean_product"), sem("var_product"), sem("gate_product")
        s_yc2, s_ysq, s_va, s_sd, s_mix = (sem("y_centred"), sem("y_squared"), sem("var"), sem("deviation"),
                                           sem("mix_ready"))
        s_xr = two("x_again")
        s_op, s_h, s_sq2, s_ms2, s_rt2, s_xn2 = (sem("out_projected"), sem("h_ready"), sem("h_squared"),
                                                 sem("h_mean_square"), sem("h_root"), sem("xn2_ready"))
        s_xw = two("xn2_written")
        s_t2, s_t2c, s_lg, s_lgu = sem("xn2_transposed"), sem("xn2T_copied"), sem("logits"), sem("logits_used")
        s_hot, s_rank, s_rku, s_slot = sem("experts_chosen"), sem("ranks"), sem("ranks_used"), sem("slots")
        s_ls, s_l0 = sem("lists_written"), sem("lists_cleared")
        s_ex2, s_g4, s_flag = sem("gate_shifted"), sem("gate_exp"), sem("flags_ready")
        s_mi = sem("moe_inputs")
        s_wt = [sem(f"expert_w{u}") for u in range(6)]
        s_ig, s_gx, s_is, s_sc = (sem("gather_list_in"), sem("tokens_gathered"), sem("scatter_list_in"),
                                  sem("rows_scattered"))
        s_xt, s_xe, s_gu, s_gd, s_g1, s_gs, s_act = (sem("xT"), sem("xT_copied"), sem("gu"), sem("gu_read"), sem("glu"),
                                                     sem("glu_sigmoid"), sem("act_ready"))
        s_dn, s_dd, s_yt, s_ye, s_l1 = sem("dn"), sem("dn_copied"), sem("y_by_token"), sem("y_rows"), sem("lin")
        s_md, s_gTc, s_bp, s_yl = (sem("experts_done"), sem("gatesT_copied"),
                                         sem("final_products"), [sem(f"pairs_in{s}") for s in range(3)])
        s_fi, s_hf, s_o, s_out = sem("final_inputs"), sem("h_final"), sem("out_ready"), two("written")
        s_fs = sem("final_step")

        NR = 2 + 3 * RT

        def weights_of(e, u):
            src = gu_w if u < 4 else dn_w
            o = u * HALF if u < 4 else (u - 4) * HALF
            return src[bass.ds(e, 1), :, o:o + HALF].rearrange("a (k p) n -> p (a k) n", p=P)

        def rounds(eng, body):
            body(0)
            eng.wait_ge(s_flag, 1)
            with eng.Fori(1, ROUNDS) as r:
                need = eng.value_load(flags[0:1, bass.ds(r, 1)], min_val=0, max_val=1)
                with eng.If(need > 0):
                    body(r)

        block = ctx.enter_context(nc.Block())

        def ring_pair(n):
            return 2 * (n % 3)

        @block.sync
        def _(sp):
            sp.dma_start(cst[:, :], consts_d[:, 0:K_MIX]).then_inc(s_par, 16)
            for t in range(2):
                sp.dma_start(xs[:, 4 * t:4 * t + 4, :], x[4 * t * P:4 * (t + 1) * P, :].rearrange("(t p) n -> p t n", p=P)
                             ).then_inc(s_x[t], 16)
            sp.dma_start(nw, normw_d[0]).then_inc(s_par, 16)
            sp.dma_start(prm[:, :], prm_d).then_inc(s_par, 16)
            sp.dma_start(lora, lora_d).then_inc(s_par, 16)
            for n in range(NR):
                if n >= 3:
                    sp.wait_ge(s_pj, 2 * (n - 2))
                sp.dma_start(win[:, n % 3, :], w_in_t[n]).then_inc(s_w[n % 3], 16)
            for j in range(3):
                sp.wait_ge(s_pj, 2 * (NR + j - 2))
                sp.dma_start(win[:, (NR + j) % 3, :], w_in_t[NR + j]).then_inc(s_wcv[j], 16)
            with sp.Fori(1, RT) as i:
                for j in range(3):
                    sp.wait_ge(s_pcv, 6 * i + 2 * j - 4)
                    sp.dma_start(win[:, (NR + j) % 3, :],
                                 w_in_t[bass.ds(NR + 3 * i + j, 1)].rearrange("a p n -> (a p) n")
                                 ).then_inc(s_wcv[j], 16)

            sp.wait_ge(s_z, 2)
            with sp.Fori(0, NCH // 2) as it:
                for s in range(2):
                    c = 2 * it + s
                    sp.wait_ge(s_y[s], it + 1)
                    sp.dma_start(ARc[s], AR[:, :, bass.ds(c, 1), :, :].rearrange("p r c k t -> p (r c) k t")
                                 ).then_inc(s_st[s], 16)
                    sp.dma_start(BKc[s], BK[:, :, bass.ds(c, 1), :, :].rearrange("p r c k t -> p (r c) k t")
                                 ).then_inc(s_st[s], 16)
                    sp.dma_start(Vc[s], V[:, :, bass.ds(c * L, L)]).then_inc(s_st[s], 16)

            sp.wait_ge(s_yc[0], NCH // 2 + 1)
            sp.wait_ge(s_yc[1], NCH // 2 + 1)
            sp.wait_ge(s_s[1], NCH // 2 + 1)
            for i in range(RT):
                sp.dma_start(bonus_in[:, i, :], bonus_d[i]).then_inc(s_pi, 16)
            sp.dma_start(wgate, wgate_d).then_inc(s_pi, 16)
            for i in range(RT):
                sp.dma_start(mixT[:, i, :], conv_d[i]).then_inc(s_wo, 16)
            sp.dma_start(wo, w_out.rearrange("(k p) n -> p k n", p=P)).then_inc(s_wo, 16)
            sp.dma_start(cst2[:, :], consts_d[:, K_MIX:NCONST]).then_inc(s_wo, 16)
            for u in range(4):
                sp.dma_start(wslot[u], weights_of(0, u)).then_inc(s_wt[u], 16)
            sp.wait_ge(s_mix, RT)
            sp.dma_start(rw, router_w.rearrange("(k p) n -> p k n", p=P)).then_inc(s_mi, 16)
            sp.dma_start(rb, router_b).then_inc(s_mi, 16)
            sp.dma_start(nw2, normw_d[1]).then_inc(s_mi, 16)
            for t in range(TT):
                if t >= 2:
                    sp.wait_ge(s_h, t - 1)
                sp.dma_start(xres[t % 2], x[t * P:(t + 1) * P, :]).then_inc(s_xr[t % 2], 16)
                if t:
                    sp.wait_ge(s_xn2, t)
                    sp.dma_start(xn_d[(t - 1) * P:t * P, :], xn2[(t - 1) % 2]).then_inc(s_xw[(t - 1) % 2], 16)
            sp.wait_ge(s_xn2, TT)
            sp.dma_start(xn_d[(TT - 1) * P:T, :], xn2[(TT - 1) % 2]).then_inc(s_xw[(TT - 1) % 2], 16)
            sp.wait_ge(s_lg, TT)
            sp.dma_start(gub, gub_d).then_inc(s_mi, 16)
            sp.wait_ge(s_xw[0], 16 * TT // 2)
            sp.wait_ge(s_xw[1], 16 * TT // 2)
            for u in (4, 5):
                sp.dma_start(wslot[u], weights_of(0, u)).then_inc(s_wt[u], 16)

            def expert_weights(lo, r):
                with sp.Fori(lo, E) as e:
                    for u in range(6):
                        n = r * E + e
                        if u < 4:
                            sp.wait_ge(s_gu, 8 * n + 2 * u - 6)
                        else:
                            sp.wait_ge(s_dn, 8 * n + 4 * u - 20)
                        sp.dma_start(wslot[u], weights_of(e, u)).then_inc(s_wt[u], 16)

            rounds(sp, lambda r: expert_weights(1 if isinstance(r, int) else 0, r))

            sp.wait_ge(s_md, 1)
            sp.dma_start(dnb[0:E, :], dn_b).then_inc(s_fi, 16)
            sp.dma_start(nw3, normw_d[2]).then_inc(s_fi, 16)
            pairs = pair_d.rearrange("(k t) n -> t k n", k=TOPK)
            for t in range(TT):
                if t >= 3:
                    sp.wait_ge(s_hf, t - 2)
                sp.dma_start(ypair[t % 3], pairs[t * P:(t + 1) * P]).then_inc(s_yl[t % 3], 16)

        @block.gpsimd
        def _(pool):
            for ahead in (*s_y, *s_yc, *s_s, s_ccp, s_u, s_cd, s_cvr, s_scr):
                pool.sem_inc(ahead, 1)
            pool.sem_inc(s_ye, 3)
            pool.dma_start(list_d, list0_d).then_inc(s_l0, 16)
            nc.gpsimd.memset(praw[:, :, 0:1], 0.0).then_inc(s_pz, 1)
            for i in range(RT - 1):
                pool.wait_ge(s_bu, i + 1)
                pool.dma_start(bonus_d[i], bonus_st[:, i % 2, :]).then_inc(s_bo[i % 2], 16)
            with pool.Fori(0, RT) as i:
                pool.wait_ge(s_cd, 2 * i + 3)
                pool.dma_start(conv_d[bass.ds(i, 1)].rearrange("a p n -> (a p) n"), conv_st[:, 0, :]).then_inc(s_cvo, 16)
                pool.wait_ge(s_cvo, 16 * i + 16)
                pool.sem_inc(s_cvr, 1)
            pool.wait_ge(s_bu, RT)
            pool.dma_start(bonus_d[RT - 1], bonus_st[:, (RT - 1) % 2, :]).then_inc(s_bo[(RT - 1) % 2], 16)
            for k in range(2):
                pool.wait_ge(s_bo[k], 16 * RT // 2)
            for s in range(2):
                for b in (MTb[s], UTb[s]):
                    last = nc.gpsimd.memset(b, 0.0)
                last.then_inc(s_z, 1)
            pool.wait_ge(s_z, 2)
            bd1 = cst[:, K_BD:K_BD + P].rearrange("p (k t) -> p k t", t=L).unsqueeze(1).to_broadcast([P, RT, 2, L])
            idb = ident.rearrange("p (k t) -> p k t", t=L).unsqueeze(1).to_broadcast([P, RT, 2, L])
            with pool.Fori(0, NCH // 2) as it:
                for s in range(2):
                    pool.wait_ge(s_mt, 2 * it + s + 1)
                    nc.gpsimd.tensor_tensor(TTb[s], MTb[s], bd1, ALU.mult).then_inc(s_tt0[s], 1)
                    pool.wait_ge(s_tt0[s], 2 * it + 1)
                    nc.gpsimd.tensor_tensor(TTb[s], TTb[s], idb, ALU.add).then_inc(s_tt0[s], 1)
            pool.wait_ge(s_l0, 16)
            for t in range(TT):
                pool.wait_ge(s_slot, t + 1)
                for k in range(TOPK):
                    pool.indirect_dma_start(list_d, bass.IndirectOffsetOnAxis(ap=slot_i[:, t, k:k + 1], axis=0),
                                            entry[:, t, k, :], None).then_inc(s_ls, 16)
            pool.wait_ge(s_ls, 16 * TT * TOPK)
            for k in range(2):
                pool.wait_ge(s_xw[k], 16 * TT // 2)
            pool.wait_ge(s_lg, TT)

            nc.gpsimd.memset(xg, 0.0)
            nc.gpsimd.memset(xg2, 0.0).then_inc(s_xz, 1)
            pool.wait_ge(s_xz, 1)

            def list_in(e, r, big, little, sem_in):
                o = e * LIST + r * C
                pool.dma_start(big[:, :], list_d[bass.ds(o, P), :]).then_inc(sem_in, 16)
                pool.dma_start(little[:, :], list_d[bass.ds(o + P, P), :]).then_inc(sem_in, 16)

            def gather(e, r, m):
                pool.wait_ge(s_gx, 32 * m)
                pool.sem_inc(s_pool_apart, 1)
                list_in(e, r, idx_g, idx_g2, s_ig)
                pool.wait_ge(s_ig, 32 * m + 32)
                pool.wait_ge(s_xt, 4 * m)
                pool.sem_inc(s_pool_apart, 1)
                pool.indirect_dma_start(xg, None, xn_d, bass.IndirectOffsetOnAxis(ap=idx_g[:, 0:1], axis=0),
                                        bounds_check=T - 1, oob_is_err=False).then_inc(s_gx, 16)
                pool.indirect_dma_start(xg2, None, xn_d, bass.IndirectOffsetOnAxis(ap=idx_g2[:, 0:1], axis=0),
                                        bounds_check=T - 1, oob_is_err=False).then_inc(s_gx, 16)

            def expert_rows(r):
                gather(0, r, r * (E + 1))
                with pool.Fori(0, E) as e:
                    n = r * E + e
                    gather(e + 1, r, r * (E + 1) + e + 1)
                    list_in(e, r, idx_s, idx_s2, s_is)
                    pool.wait_ge(s_is, 32 * n + 32)
                    pool.wait_ge(s_ye, 4 * n + 7)
                    pool.sem_inc(s_pool_apart, 1)
                    pool.indirect_dma_start(pair_d, bass.IndirectOffsetOnAxis(ap=idx_s[:, 1:2], axis=0), Yt, None,
                                            bounds_check=PAIRS - 1, oob_is_err=False).then_inc(s_sc, 16)
                    pool.indirect_dma_start(pair_d, bass.IndirectOffsetOnAxis(ap=idx_s2[:, 1:2], axis=0), Y2, None,
                                            bounds_check=PAIRS - 1, oob_is_err=False).then_inc(s_sc, 16)
                    pool.wait_ge(s_sc, 32 * n + 32)
                    pool.sem_inc(s_scr, 1)

            rounds(pool, expert_rows)
            pool.sem_inc(s_md, 1)

        @block.scalar
        def _(act):
            for t in range(TT):
                act.wait_ge(s_x[t // 4], 16)
                if t:
                    act.wait_ge(s_sq, t)
                nc.scalar.activation(sqj, xs[:, t, :], ACT.Square, accum_out=stat[:, 0, t:t + 1]).then_inc(s_sq, 1)
            act.wait_ge(s_ms, 1)
            nc.scalar.activation(stat[:, 1, :], stat[:, 1, :], ACT.Sqrt).then_inc(s_rt, 1)
            for t in range(TT):
                act.wait_ge(s_tr, 2 * t + 1)
                nc.scalar.copy(xnT[:, 0:4, t * P:(t + 1) * P],
                               ps[:, 2 * (t % 2), :].rearrange("p (k t) -> p k t", t=P)).then_inc(s_te, 1)
            def copy_raw(n):
                for h in range(2):
                    act.wait_ge(s_pj, 2 * n + h + 1)
                    if h == 0 and n >= 2:
                        act.wait_ge(s_pu, n - 1)
                    nc.scalar.copy(praw[:, n % 2, 1 + h * HALF:1 + (h + 1) * HALF],
                                   ps[:, ring_pair(n) + h, :]).then_inc(s_pc, 1)
            copy_raw(0)
            copy_raw(1)
            act.wait_ge(s_pu, 1)
            nc.scalar.activation(tdwa[0:LORA, :], tdwa[0:LORA, :], ACT.Tanh).then_inc(s_lo, 1)
            act.wait_ge(s_pu, 2)
            nc.scalar.activation(sdg, sdg, ACT.Sigmoid).then_inc(s_lo, 1)
            for i in range(RT):
                n = 2 + 3 * i
                copy_raw(n)
                for h in range(2):
                    act.wait_ge(s_pm, 8 * i + h + 1)
                    if h == 0 and i:
                        act.wait_ge(s_td, i)
                    nc.scalar.activation(W1[:, h * HALF:(h + 1) * HALF], ps[:, 6 + h, :], ACT.Sigmoid,
                                         bias=prm[:, W0 + i:W0 + i + 1]).then_inc(s_sg, 1)
                copy_raw(n + 1)
                for h in range(2):
                    act.wait_ge(s_pm, 8 * i + 2 + h + 1)
                    nc.scalar.activation(W4[:, h * HALF:(h + 1) * HALF], ps[:, 6 + h, :], ACT.Sigmoid,
                                         bias=prm[:, A0 + i:A0 + i + 1]).then_inc(s_sg, 1)
                act.wait_ge(s_cu, i + 1)
                nc.scalar.activation(W3, W2, ACT.Exp, scale=-KAPPA).then_inc(s_ex, 1)
                nc.scalar.activation(W1, W1, ACT.Exp, scale=-KAPPA).then_inc(s_ex, 1)
                act.wait_ge(s_ex, 3 * i + 1)
                nc.scalar.activation(W2, W2, ACT.Exp, scale=KAPPA).then_inc(s_ex, 1)
                act.wait_ge(s_kk, i + 1)
                if i:
                    act.wait_ge(s_bu, i)
                nc.scalar.activation(W8, W7, ACT.Square).then_inc(s_sk, 1)
                copy_raw(n + 2)
                for h in range(2):
                    act.wait_ge(s_pm, 8 * i + 4 + h + 1)
                    nc.scalar.activation(W8[:, h * HALF:(h + 1) * HALF], ps[:, 6 + h, :], ACT.Sqrt).then_inc(s_nr, 1)
            with act.Fori(0, RT) as i:
                for h in range(2):
                    act.wait_ge(s_pcv, 6 * i + h + 1)
                    if h == 0:
                        act.wait_ge(s_u, 2 * i + 1)
                        act.wait_ge(s_td, RT)
                        act.wait_ge(s_pu, NR)
                    nc.scalar.copy(ccs[:, h * HALF:(h + 1) * HALF], ps[:, ring_pair(NR) + h, :]).then_inc(s_ccp, 1)

            lo, hi = slice(0, N), slice(N, P)
            act.wait_ge(s_z, 2)
            with act.Fori(0, NCH // 2) as it:
                for s in range(2):
                    b = 4 * s
                    act.wait_ge(s_gm[s], 2 * it + 2)
                    gm = Gm[s].rearrange("p (r h) q -> p r h q", h=2)
                    nc.scalar.copy(MTb[s][lo, :, 0, :], gm[lo, :, 0, 0:L])
                    nc.scalar.copy(MTb[s][hi, :, 1, :], gm[hi, :, 1, 0:L]).then_inc(s_mt, 1)
                    act.wait_ge(s_v, 2 * it + s + 1)
                    vq = ps[:, b + 3, 0:RT * L].rearrange("p (r i) -> p r i", i=L)
                    sv = SAV[s].rearrange("p (r h) i -> p r h i", h=2)
                    nc.scalar.copy(sv[hi, :, 0, :], vq[hi])
                    nc.scalar.copy(sv[lo, :, 1, :], vq[lo])
                    act.wait_ge(s_m, 2 * it + s + 1)
                    nc.scalar.copy(MAt[s], ps[:, b + 2, :].rearrange("p (k r i) -> p k r i", k=2, r=RT)
                                   ).then_inc(s_ac, 1)
                for s in range(2):
                    act.wait_ge(s_bt, 2 * it + s + 1)
                    bt = BKt[s].rearrange("p (r h) i -> p r h i", h=2)
                    for h in range(2):
                        nc.scalar.copy(bt[:, :, h, :], ps[:, 4 * s + 3 - h, 0:RT * L].rearrange("p (r i) -> p r i", i=L)
                                       ).then_inc(s_bc[s], 1)
                for s in range(2):
                    b = 4 * s
                    act.wait_ge(s_nv, 2 * it + s + 1)
                    nc.scalar.copy(NVs[s], ps[:, b + 3, 0:RT * L].rearrange("p (r i) -> p r i", i=L)).then_inc(s_nvc, 1)
                for s in range(2):
                    b = 4 * s
                    act.wait_ge(s_ut, 2 * it + s + 1)
                    uq = ps[:, b + 3, 0:RT * L].rearrange("p (r i) -> p r i", i=L)
                    nc.scalar.copy(UTb[s][lo, :, 0, :], uq[lo])
                    nc.scalar.copy(UTb[s][hi, :, 1, :], uq[hi]).then_inc(s_utc, 1)
                for s in range(2):
                    act.wait_ge(s_y[s], it + 2)
                    nc.scalar.copy(YF[:, :, bass.ds((2 * it + s) * L, L)],
                                   ps[:, 4 * s + 1, 0:RT * L].rearrange("p (r i) -> p r i", i=L)).then_inc(s_yc[s], 1)
            for i in range(RT):
                act.wait_ge(s_yc2, 2 * i + 2)
                nc.scalar.activation(gn_sq[i % 2], gn_yc[i % 2], ACT.Square).then_inc(s_ysq, 1)
                for h in range(2):
                    act.wait_ge(s_vp, 2 * i + h + 1)
                    nc.scalar.activation(gn_sd[i % 2][:, h * HALF:(h + 1) * HALF], ps[:, 2 + h, :], ACT.Ln,
                                         bias=gneps[:, :], scale=1.0 / N).then_inc(s_va, 1)
                act.wait_ge(s_va, 2 * i + 2)
                nc.scalar.activation(gn_sd[i % 2], gn_sd[i % 2], ACT.Exp, scale=-0.5).then_inc(s_sd, 1)
            for t in range(TT + 1):
                if t:
                    u = t - 1
                    for g in range(2):
                        act.wait_ge(s_t2, 2 * u + g + 1)
                        nc.scalar.copy(xn2T[u % 2][:, 4 * g:4 * g + 4, :],
                                       ps[:, 4 + g, :].rearrange("p (k t) -> p k t", t=P)).then_inc(s_t2c, 1)
                if t < TT:
                    act.wait_ge(s_h, t + 1)
                    if t:
                        act.wait_ge(s_sq2, t)
                    nc.scalar.activation(sqj2, h_sb[:, t, :], ACT.Square, accum_out=stat2[:, 0, t:t + 1]
                                         ).then_inc(s_sq2, 1)
                    act.wait_ge(s_ms2, t + 1)
                    nc.scalar.activation(stat2[:, 1, t:t + 1], stat2[:, 1, t:t + 1], ACT.Sqrt).then_inc(s_rt2, 1)
                if t:
                    act.wait_ge(s_ex2, t)
                    nc.scalar.activation(gates[:, t - 1, :], gates[:, t - 1, :], ACT.Exp, accum_out=gsum[:, t - 1:t]
                                         ).then_inc(s_g4, 1)

            def copy_xT(m, quarters):
                for q in quarters:
                    act.wait_ge(s_xt, 4 * m + q + 1)
                    nc.scalar.copy(xT[:, 2 * q:2 * q + 2, :], ps[:, 4 + q % 2, :].rearrange("p (k c) -> p k c", c=C)
                                   ).then_inc(s_xe, 1)

            def expert_act(r):
                copy_xT(r * (E + 1), range(4))
                with act.Fori(0, E) as e:
                    n = r * E + e
                    for f in range(KT):
                        act.wait_ge(s_g1, 8 * n + f + 1)
                        nc.scalar.activation(sgm[f % 2], gt[f % 2], ACT.Sigmoid, scale=ALPHA).then_inc(s_gs, 1)
                    copy_xT(r * (E + 1) + e + 1, (0, 1))
                    for d in range(KT):
                        act.wait_ge(s_dn, 8 * n + d + 1)
                        nc.scalar.copy(yT[:, d, :], ps[:, 2 + d % 2, 0:C]).then_inc(s_dd, 1)
                    copy_xT(r * (E + 1) + e + 1, (2, 3))

            rounds(act, expert_act)
            act.wait_ge(s_md, 1)
            act.wait_ge(s_bp, 1)
            nc.scalar.copy(GT[0:E, 0:4, :], ps[0:E, 0, :].rearrange("p (k t) -> p k t", t=P))
            nc.scalar.copy(GT[0:E, 4:8, :], ps[0:E, 1, :].rearrange("p (k t) -> p k t", t=P)).then_inc(s_gTc, 1)
            for t in range(TT + 1):
                if t < TT:
                    act.wait_ge(s_hf, t + 1)
                    act.wait_ge(s_sq2, TT + t)
                    nc.scalar.activation(sqj3, h_sb[:, t, :], ACT.Square, accum_out=stat3[:, 0, t:t + 1]
                                         ).then_inc(s_sq2, 1)
                    act.wait_ge(s_ms2, TT + t + 1)
                    nc.scalar.activation(stat3[:, 1, t:t + 1], stat3[:, 1, t:t + 1], ACT.Sqrt).then_inc(s_rt2, 1)
                if t:
                    act.wait_ge(s_o, t)
                    act.dma_start(out[(t - 1) * P:t * P, :], fin[(t - 1) % 2]).then_inc(s_out[(t - 1) % 2], 16)
            for k in range(2):
                act.wait_ge(s_out[k], 16 * TT // 2)

        @block.vector
        def _(dve):
            ch = Chain(dve, s_dv)
            dve.wait_ge(s_sq, TT)
            nc.vector.tensor_scalar(stat[:, 1, :], stat[:, 0, :], 1.0 / D, RMS_EPS, ALU.mult, ALU.add).then_inc(s_ms, 1)
            dve.wait_ge(s_rt, 1)
            ch.link(nc.vector.reciprocal(stat[:, 2, :], stat[:, 1, :]))
            dve.wait_ge(s_par, 4 * 16)
            for t in range(TT):
                nc.vector.scalar_tensor_tensor(out=xs[:, t, :], in0=xs[:, t, :], scalar=stat[:, 2, t:t + 1],
                                               in1=nw, op0=ALU.mult, op1=ALU.mult).then_inc(s_xn, 1)
            for t in range(TT):
                dve.wait_ge(s_tr, 2 * t + 2)
                nc.vector.tensor_copy(xnT[:, 4:8, t * P:(t + 1) * P],
                                      ps[:, 2 * (t % 2) + 1, :].rearrange("p (k t) -> p k t", t=P)).then_inc(s_tv, 1)
            ch.link(nc.vector.tensor_scalar(omka[:, :], prm[:, KAW:KAW + RT], -1.0, 1.0, ALU.mult, ALU.add))

            def shift(n, dst, wait=None):
                dve.wait_ge(s_pc, 2 * n + 2)
                if n == 0:
                    dve.wait_ge(s_pz, 1)
                now, past = praw[:, n % 2, 1:1 + T], praw[:, n % 2, 0:T]
                ch.link(nc.vector.tensor_tensor(W6, past, now, ALU.subtract))
                mu = {0: 12, 1: 13}.get(n, (n - 2) % 3 * RT + (n - 2) // 3)
                nc.vector.scalar_tensor_tensor(out=dst, in0=W6, scalar=prm[:, MU + mu:MU + mu + 1], in1=now,
                                               op0=ALU.mult, op1=ALU.add).then_inc(s_pu, 1)
                dve.wait_ge(s_pu, n + 1)

            shift(0, tdwa)
            shift(1, sdg)

            def bonus_product(i):
                dve.wait_ge(s_pm, 8 * i + 8)
                if i >= 2:
                    dve.wait_ge(s_bo[i % 2], 16 * (i // 2))
                nc.vector.tensor_tensor(bonus_st[:, i % 2, 0:HALF], ps[:, 6, :], V[:, i, 0:HALF], ALU.mult)
                nc.vector.tensor_tensor(bonus_st[:, i % 2, HALF:T], ps[:, 7, :], V[:, i, HALF:T],
                                        ALU.mult).then_inc(s_bu, 1)

            for i in range(RT):
                n = 2 + 3 * i
                if i:
                    bonus_product(i - 1)
                shift(n, q_r)
                dve.wait_ge(s_sg, 4 * i + 2)
                for c in range(NCH):
                    w = slice(c * L, (c + 1) * L)
                    last = nc.vector.tensor_tensor_scan(W2[:, w], W1[:, w], W1[:, w], 0.0, ALU.add, ALU.max)
                ch.link(last)
                nc.vector.tensor_tensor(W1, W2, W1, ALU.subtract).then_inc(s_cu, 1)
                shift(n + 1, q_k)
                nc.vector.tensor_scalar(W7, q_k, prm[:, KKW + i:KKW + i + 1], None, ALU.mult).then_inc(s_kk, 1)
                dve.wait_ge(s_ex, 3 * i + 1)
                nc.vector.tensor_tensor(AR[:, i, :, 1, :], q_r.rearrange("p (c t) -> p c t", t=L),
                                        W3.rearrange("p (c t) -> p c t", t=L), ALU.mult)
                nc.vector.tensor_copy(cL[:, i, :], W3.rearrange("p (c t) -> p c t", t=L)[:, :, L - 1])
                dve.wait_ge(s_sg, 4 * i + 4)
                ch.link(nc.vector.tensor_scalar(W6, W4, prm[:, KAW + i:KAW + i + 1], omka[:, i:i + 1], ALU.mult, ALU.add))
                ch.link(nc.vector.tensor_tensor(q_k, q_k, W6, ALU.mult))
                dve.wait_ge(s_ex, 3 * i + 3)
                cv = [a.rearrange("p (c t) -> p c t", t=L) for a in (W4, q_k, W2, W1, W7)]
                lo, hi = slice(0, N), slice(N, P)
                nc.vector.tensor_tensor(BK[lo, i, :, 1, :], cv[1][lo], cv[2][lo], ALU.mult)
                nc.vector.tensor_tensor(BK[hi, i, :, 0, :], cv[1][hi], cv[2][hi], ALU.mult)
                dve.wait_ge(s_nr, 2 * i + 2)
                ch.link(nc.vector.tensor_scalar(W8, W8, 1e-12, None, ALU.max))
                ch.link(nc.vector.reciprocal(W8, W8))
                ch.link(nc.vector.tensor_tensor(W7, W7, W8, ALU.mult))
                ch.link(nc.vector.tensor_tensor(W4, W4, W7, ALU.mult))
                nc.vector.scalar_tensor_tensor(out=W8, in0=q_r, scalar=prm[:, RKW + i:RKW + i + 1], in1=q_k,
                                               op0=ALU.mult, op1=ALU.mult).then_inc(s_rk, 1)
                nc.vector.tensor_tensor(BK[lo, i, :, 0, :], cv[0][lo], cv[2][lo], ALU.mult)
                nc.vector.tensor_tensor(BK[hi, i, :, 1, :], cv[0][hi], cv[2][hi], ALU.mult)
                nc.vector.scalar_tensor_tensor(out=AR[:, i, :, 0, :], in0=cv[4], scalar=-1.0, in1=cv[3],
                                               op0=ALU.mult, op1=ALU.mult).then_inc(s_td, 1)
                shift(n + 2, V[:, i, :])
            ch.link(nc.vector.memset(u_cv[:, 0:2], 0.0))
            with dve.Fori(0, RT) as i:
                cc = Chain(dve, s_cds, i * 3)
                w = [prm[:, bass.ds(CVW + i * 3 + j, 1)] for j in range(3)]
                for h in range(2):
                    dve.wait_ge(s_ccp, 2 * i + h + 2)
                    dve.wait_ge(s_pcv, 6 * i + 2 + h + 1)
                    nc.vector.tensor_tensor(u_cv[:, 2 + h * HALF:2 + (h + 1) * HALF], ccs[:, h * HALF:(h + 1) * HALF],
                                            ps[:, ring_pair(NR + 1) + h, :], ALU.mult).then_inc(s_u, 1)
                dve.wait_ge(s_u, 2 * i + 3)
                cc.link(nc.vector.tensor_scalar(t_cv, u_cv[:, 0:T], w[0], None, ALU.mult))
                cc.link(nc.vector.scalar_tensor_tensor(out=t_cv, in0=u_cv[:, 1:1 + T], scalar=w[1], in1=t_cv,
                                                       op0=ALU.mult, op1=ALU.add))
                cc.link(nc.vector.scalar_tensor_tensor(out=t_cv, in0=u_cv[:, 2:2 + T], scalar=w[2], in1=t_cv,
                                                       op0=ALU.mult, op1=ALU.add))
                for h in range(2):
                    dve.wait_ge(s_pcv, 6 * i + 4 + h + 1)
                    dve.wait_ge(s_cvr, i + 1)
                    nc.vector.tensor_tensor(conv_st[:, 0, h * HALF:(h + 1) * HALF], t_cv[:, h * HALF:(h + 1) * HALF],
                                            ps[:, ring_pair(NR + 2) + h, :], ALU.mult).then_inc(s_cd, 1)
            bonus_product(RT - 1)

            lo, hi = slice(0, N), slice(N, P)
            dve.wait_ge(s_z, 2)
            nc.vector.memset(gneps[:, :], GN_EPS)
            nc.vector.memset(St[0], 0.0).then_inc(s_zv, 1)
            dve.wait_ge(s_zv, 1)
            mg = cst[:, K_MG:K_MG + P].unsqueeze(1).to_broadcast([P, RT, P])
            m1 = cst[:, K_M1:K_M1 + L].unsqueeze(1).to_broadcast([P, RT, L])
            i2 = cst[:, K_ID2:K_ID2 + L].unsqueeze(1).to_broadcast([P, RT, L])
            with dve.Fori(0, NCH // 2) as it:
                cc = Chain(dve, s_cst, it * 2)
                for s in range(2):
                    b = 4 * s
                    dve.wait_ge(s_st[s], 48 * it + 48)
                    if s == 0:
                        dve.wait_ge(s_s[1], it + 1)
                    decay = cL[:, :, bass.ds(2 * it + s, 1)].unsqueeze(3).to_broadcast([P, RT, 1, 2 * L])
                    nc.vector.tensor_tensor(BKs[s].rearrange("p r k t -> p r (k t)").unsqueeze(2),
                                            BKc[s].rearrange("p r k t -> p r (k t)").unsqueeze(2),
                                            decay, ALU.mult).then_inc(s_bs, 1)
                    dve.wait_ge(s_g, 2 * it + s + 1)
                    for g in range(2):
                        nc.vector.tensor_tensor(Gm[s].rearrange("p (r h) q -> p h r q", h=2)[:, g, :, :],
                                                ps[:, b + g, :].rearrange("p (h q) -> p h q", q=P), mg,
                                                ALU.mult).then_inc(s_gm[s], 1)
                    dve.wait_ge(s_ac, 2 * it + s + 1)
                    cc.link(nc.vector.tensor_tensor(Tst[s], MAt[s][:, 0], m1, ALU.mult))
                    nc.vector.tensor_tensor(Tst[s], Tst[s], i2, ALU.add).then_inc(s_t[s], 1)
                for l in range(len(LEVELS)):
                    me = cst[:, K_ME + l * L:K_ME + (l + 1) * L].unsqueeze(1).to_broadcast([P, RT, L])
                    mb = (cst[:, K_MTB + l * P:K_MTB + (l + 1) * P].rearrange("p (k t) -> p k t", t=L)
                          .unsqueeze(1).to_broadcast([P, RT, 2, L]))
                    for s in range(2):
                        b = 4 * s
                        eq = ps[:, b, 0:RT * L].rearrange("p (r i) -> p r i", i=L)
                        dve.wait_ge(s_pe_e[s], 5 * it + l + 1)
                        nc.vector.tensor_tensor(Est[s], eq, me, ALU.mult).then_inc(s_e[s], 1)
                        nc.vector.tensor_tensor(Ebd[s], eq.unsqueeze(2).to_broadcast([P, RT, 2, L]), mb,
                                                ALU.mult).then_inc(s_e[s], 1)
                    for s in range(2):
                        b = 4 * s
                        if l < 4:
                            dve.wait_ge(s_pe_f[s], 4 * it + l + 1)
                            dve.wait_ge(s_t[s], 5 * it + l + 1)
                            nc.vector.tensor_tensor(Tst[s], ps[:, b + 2, 0:RT * L].rearrange("p (r i) -> p r i", i=L),
                                                    Tst[s], ALU.add).then_inc(s_t[s], 1)
                        dve.wait_ge(s_pe_ft[s], 5 * it + l + 1)
                        if l:
                            dve.wait_ge(s_tt[s], 5 * it + l)
                        else:
                            dve.wait_ge(s_tt0[s], 2 * it + 2)
                        nc.vector.tensor_tensor(TTb[s], ps[:, b + 1, :].rearrange("p (r k t) -> p r k t", k=2, t=L),
                                                TTb[s], ALU.add).then_inc(s_tt[s], 1)
                for s in range(2):
                    b = 4 * s
                    if s == 0:
                        dve.wait_ge(s_s[1], it + 1)
                    else:
                        dve.wait_ge(s_s[0], it + 2)
                    decay = cL[:, :, bass.ds(2 * it + s, 1)].to_broadcast([P, RT, L])
                    nc.vector.tensor_tensor(Sc, St[s], decay, ALU.mult).then_inc(s_zv, 1)
                    dve.wait_ge(s_sa, 2 * it + s + 1)
                    aq = ps[:, b + 2, 0:RT * L].rearrange("p (r i) -> p r i", i=L)
                    sv = SAV[s].rearrange("p (r h) i -> p r h i", h=2)
                    nc.vector.tensor_copy(sv[lo, :, 0, :], aq[lo])
                    nc.vector.tensor_copy(sv[hi, :, 1, :], aq[hi]).then_inc(s_sac, 1)
                    dve.wait_ge(s_zv, 2 * it + s + 2)
                    dve.wait_ge(s_sn, 2 * it + s + 1)
                    if s == 1:
                        dve.wait_ge(s_y[0], it + 2)
                    else:
                        dve.wait_ge(s_y[1], it + 1)
                    nc.vector.tensor_tensor(St[1 - s], ps[:, b + 3, 0:RT * L].rearrange("p (r i) -> p r i", i=L),
                                            Sc, ALU.add).then_inc(s_s[s], 1)

            dve.wait_ge(s_pi, 16 * (RT + 1))
            for i in range(RT):
                yc, sd = gn_yc[i % 2], gn_sd[i % 2]
                for h in range(2):
                    w = slice(h * HALF, (h + 1) * HALF)
                    dve.wait_ge(s_mp, 2 * i + h + 1)
                    nc.vector.scalar_tensor_tensor(out=yc[:, w], in0=ps[:, h, :], scalar=-1.0 / N, in1=YF[:, i, w],
                                                   op0=ALU.mult, op1=ALU.add).then_inc(s_yc2, 1)
                dve.wait_ge(s_sd, i + 1)
                ch.link(nc.vector.tensor_tensor(yc, yc, sd, ALU.mult))
                ch.link(nc.vector.tensor_scalar(yc, yc, prm[:, LNW + i:LNW + i + 1], prm[:, LNB + i:LNB + i + 1],
                                                ALU.mult, ALU.add))
                ch.link(nc.vector.tensor_tensor(yc, yc, bonus_in[:, i, :], ALU.add))
                dve.wait_ge(s_gp, 2 * i + 2)
                nc.vector.tensor_tensor(mixT[:, RT + i, 0:HALF], yc[:, 0:HALF], ps[:, 4, :], ALU.mult)
                nc.vector.tensor_tensor(mixT[:, RT + i, HALF:T], yc[:, HALF:T], ps[:, 5, :], ALU.mult).then_inc(s_mix, 1)

            dve.wait_ge(s_wo, 16 * (RT + 2))
            dve.wait_ge(s_mi, 3 * 16)
            ch.link(nc.vector.memset(seen[:, :], 0.0))
            ch.link(nc.vector.tensor_scalar(desc[:, :], iexp, -1.0, float(E), ALU.mult, ALU.add))
            ch.link(nc.vector.tensor_scalar(eoff[:, :], iexp, float(LIST), None, ALU.mult))
            for t in range(TT + 2):
                if t < TT:
                    dve.wait_ge(s_xr[t % 2], 16 * (t // 2 + 1))
                    dve.wait_ge(s_op, 2 * t + 2)
                    b = 2 * (t % 2)
                    nc.vector.tensor_tensor(h_sb[:, t, 0:HALF], ps[:, b, :], xres[t % 2][:, 0:HALF], ALU.add)
                    nc.vector.tensor_tensor(h_sb[:, t, HALF:D], ps[:, b + 1, :], xres[t % 2][:, HALF:D],
                                            ALU.add).then_inc(s_h, 1)
                    dve.wait_ge(s_sq2, t + 1)
                    nc.vector.tensor_scalar(stat2[:, 1, t:t + 1], stat2[:, 0, t:t + 1], 1.0 / D, RMS_EPS,
                                            ALU.mult, ALU.add).then_inc(s_ms2, 1)
                    dve.wait_ge(s_rt2, t + 1)
                    ch.link(nc.vector.reciprocal(stat2[:, 2, t:t + 1], stat2[:, 1, t:t + 1]))
                    if t >= 2:
                        dve.wait_ge(s_xw[t % 2], 16 * (t // 2))
                        dve.wait_ge(s_t2, 2 * t - 2)
                    nc.vector.scalar_tensor_tensor(out=xn2[t % 2], in0=h_sb[:, t, :], scalar=stat2[:, 2, t:t + 1],
                                                   in1=nw2, op0=ALU.mult, op1=ALU.mult).then_inc(s_xn2, 1)
                if t >= 2:
                    u = t - 2
                    one_hot, chosen = hot4[u % 2], hots[u % 2]
                    dve.wait_ge(s_g4, u + 1)
                    ch.link(nc.vector.reciprocal(gsum[:, u:u + 1], gsum[:, u:u + 1]))
                    ch.link(nc.vector.tensor_scalar(gates[:, u, :], gates[:, u, :], gsum[:, u:u + 1], None, ALU.mult))
                    ch.link(nc.vector.tensor_scalar(G[:, u, :], one_hot[:, 0, :], gates[:, u, 0:1], None, ALU.mult))
                    for k in range(1, TOPK):
                        ch.link(nc.vector.scalar_tensor_tensor(out=G[:, u, :], in0=one_hot[:, k, :],
                                                               scalar=gates[:, u, k:k + 1], in1=G[:, u, :],
                                                               op0=ALU.mult, op1=ALU.add))
                    dve.wait_ge(s_rank, u + 1)
                    ch.link(nc.vector.tensor_tensor(rk, ps[:, 7, 0:E], seen[:, :], ALU.add))
                    nc.vector.tensor_tensor(seen[:, :], ps[:, 7, E:2 * E], seen[:, :], ALU.add).then_inc(s_rku, 1)
                    ch.link(nc.vector.tensor_tensor(rk, rk, eoff[:, :], ALU.add))
                    for k in range(TOPK):
                        ch.link(nc.vector.tensor_tensor(prod, one_hot[:, k, :], rk, ALU.mult))
                        ch.link(nc.vector.reduce_sum(slot_f[:, k:k + 1], prod, AX.X))
                        nc.vector.tensor_copy(entry[:, u, k, 0:1], itok[:, u:u + 1])
                        nc.vector.tensor_scalar(entry[:, u, k, 1:2], itok[:, u:u + 1], float(k * T), None, ALU.add)
                    nc.vector.tensor_copy(slot_i[:, u, :], slot_f[:, :]).then_inc(s_slot, 1)
                if 1 <= t <= TT:
                    u = t - 1
                    one_hot, chosen = hot4[u % 2], hots[u % 2]
                    dve.wait_ge(s_lg, u + 1)
                    nc.vector.tensor_tensor(lg, ps[:, 6, 0:E], rb, ALU.add).then_inc(s_lgu, 1)
                    dve.wait_ge(s_lgu, u + 1)
                    for k in range(TOPK):
                        ch.link(nc.vector.reduce_max(topv[:, u, k:k + 1], lg, AX.X))
                        ch.link(nc.vector.scalar_tensor_tensor(out=hot, in0=lg, scalar=topv[:, u, k:k + 1],
                                                               in1=desc[:, :], op0=ALU.is_equal, op1=ALU.mult))
                        ch.link(nc.vector.reduce_max(small[:, 0:1], hot, AX.X))
                        ch.link(nc.vector.tensor_scalar(one_hot[:, k, :], desc[:, :], small[:, 0:1], None, ALU.is_equal))
                        if k < TOPK - 1:
                            ch.link(nc.vector.scalar_tensor_tensor(out=lg, in0=one_hot[:, k, :], scalar=-3e38, in1=lg,
                                                                   op0=ALU.mult, op1=ALU.add))
                    nc.vector.tensor_scalar(gates[:, u, :], topv[:, u, :], topv[:, u, 0:1], None, ALU.subtract
                                            ).then_inc(s_ex2, 1)
                    ch.link(nc.vector.tensor_tensor(chosen, one_hot[:, 0, :], one_hot[:, 1, :], ALU.add))
                    ch.link(nc.vector.tensor_tensor(prod, one_hot[:, 2, :], one_hot[:, 3, :], ALU.add))
                    nc.vector.tensor_tensor(chosen, chosen, prod, ALU.add).then_inc(s_hot, 1)
            ch.link(nc.vector.reduce_max(small[:, 1:2], seen[:, :], AX.X))
            nc.vector.tensor_scalar(flags[:, :], iexp[:, 0:8], float(C), small[:, 1:2], ALU.mult, ALU.is_lt
                                    ).then_inc(s_flag, 1)
            for r in range(ROUNDS):
                ch.link(nc.vector.tensor_scalar(left, seen[:, :], float(-r * C), None, ALU.add))
                ch.link(nc.vector.tensor_scalar(size_f[:, r, :], left, float(SIZES[0]), None, ALU.is_gt))
                for z in SIZES[1:-1]:
                    ch.link(nc.vector.scalar_tensor_tensor(out=size_f[:, r, :], in0=left, scalar=float(z),
                                                           in1=size_f[:, r, :], op0=ALU.is_gt, op1=ALU.add))
            nc.vector.tensor_copy(size_i[:, :], size_f.rearrange("p r e -> p (r e)")).then_inc(s_sz, 1)
            dve.wait_ge(s_mi, 4 * 16)
            ch.link(nc.vector.tensor_scalar(gub1, gub, 1.0, None, ALU.add))

            def expert_dve(r):
                with dve.Fori(0, E) as e:
                    n = r * E + e
                    for f in range(KT):
                        b = f % 2
                        dve.wait_ge(s_gu, 8 * n + f + 1)
                        nc.vector.tensor_scalar(gt[b], ps[:, b, 0:C], gub[:, bass.ds(e * 16 + 2 * f, 1)], LIMIT,
                                                ALU.add, ALU.min).then_inc(s_g1, 1)
                        nc.vector.tensor_scalar(lt[b], ps[:, b, C:2 * C], gub1[:, bass.ds(e * 16 + 2 * f + 1, 1)],
                                                LIMIT + 1, ALU.add, ALU.min).then_inc(s_gd, 1)
                        dve.wait_ge(s_gd, 8 * n + f + 1)
                        dve.wait_ge(s_gs, 8 * n + f + 1)
                        nc.vector.scalar_tensor_tensor(out=lt[b], in0=lt[b], scalar=1 - LIMIT, in1=sgm[b],
                                                       op0=ALU.max, op1=ALU.mult).then_inc(s_l1, 1)
                        dve.wait_ge(s_l1, 8 * n + f + 1)
                        nc.vector.tensor_tensor(actT[:, f, :], lt[b], gt[b], ALU.mult).then_inc(s_act, 1)
                    for q in range(4):
                        dve.wait_ge(s_yt, 4 * n + q + 1)
                        if q == 0:
                            dve.wait_ge(s_scr, n + 1)
                        half = q // 2
                        rows, bank = ((Yt, 6 + half), (Y2, half))[q % 2]
                        nc.vector.tensor_copy(rows[:, half * HALF:(half + 1) * HALF], ps[:, bank, :]).then_inc(s_ye, 1)

            rounds(dve, expert_dve)

            dve.wait_ge(s_md, 1)
            for t in range(TT):
                last = nc.vector.tensor_scalar(dgate[:, t, :], ident, gates[:, t, 0:1], None, ALU.mult)
            last.then_inc(s_fs, 1)
            dve.wait_ge(s_fi, 32)
            for t in range(TT + 1):
                if t < TT:
                    b = 2 + 2 * (t % 2)
                    for h in range(2):
                        dve.wait_ge(s_bp, 2 * t + h + 2)
                        w = slice(h * HALF, (h + 1) * HALF)
                        nc.vector.tensor_tensor(h_sb[:, t, w], ps[:, b + h, :], h_sb[:, t, w], ALU.add).then_inc(s_fs, 1)
                if t:
                    u = t - 1
                    dve.wait_ge(s_sq2, TT + u + 1)
                    nc.vector.tensor_scalar(stat3[:, 1, u:u + 1], stat3[:, 0, u:u + 1], 1.0 / D, RMS_EPS,
                                            ALU.mult, ALU.add).then_inc(s_ms2, 1)
                if t < TT:
                    dve.wait_ge(s_yl[t % 3], 16 * (t // 3 + 1))
                    for k in range(1, TOPK):
                        dve.wait_ge(s_fs, 4 * t + k + 2)
                        nc.vector.scalar_tensor_tensor(out=h_sb[:, t, :], in0=ypair[t % 3][:, k, :],
                                                       scalar=gates[:, t, k:k + 1], in1=h_sb[:, t, :],
                                                       op0=ALU.mult, op1=ALU.add
                                                       ).then_inc(s_fs if k < TOPK - 1 else s_hf, 1)
                if t:
                    dve.wait_ge(s_rt2, TT + u + 1)
                    ch.link(nc.vector.reciprocal(stat3[:, 2, u:u + 1], stat3[:, 1, u:u + 1]))
                    if u >= 2:
                        dve.wait_ge(s_out[u % 2], 16 * (u // 2))
                    nc.vector.scalar_tensor_tensor(out=fin[u % 2], in0=h_sb[:, u, :], scalar=stat3[:, 2, u:u + 1],
                                                   in1=nw3, op0=ALU.mult, op1=ALU.mult).then_inc(s_o, 1)

        @block.tensor
        def _(pe):
            pe.wait_ge(s_par, 4 * 16)
            for t in range(TT):
                pe.wait_ge(s_xn, t + 1)
                for g in range(2):
                    if t >= 2:
                        pe.wait_ge((s_te, s_tv)[g], t - 1)
                    for k in range(4):
                        kt = 4 * g + k
                        last = nc.tensor.transpose(ps[:, 2 * (t % 2) + g, k * P:(k + 1) * P],
                                                   xs[:, t, kt * P:(kt + 1) * P], ident)
                    last.then_inc(s_tr, 1)
            pe.wait_ge(s_te, TT)
            pe.wait_ge(s_tv, TT)

            def project(slot, bank, h):
                for kt in range(KT):
                    last = nc.tensor.matmul(ps[:, bank + h, :], win[:, slot, kt * P:(kt + 1) * P],
                                            xnT[:, kt, h * HALF:(h + 1) * HALF], start=kt == 0, stop=kt == KT - 1)
                return last

            def tile(n, between=None):
                pe.wait_ge(s_w[n % 3], 16 * (n // 3 + 1))
                for h in range(2):
                    if n >= 3:
                        pe.wait_ge(s_pc, 2 * (n - 3) + h + 1)
                    project(n % 3, ring_pair(n), h).then_inc(s_pj, 1)
                    if h == 0 and between is not None:
                        between()

            def bonus(i):
                def go():
                    pe.wait_ge(s_rk, i + 1)
                    for h in range(2):
                        nc.tensor.matmul(ps[:, 6 + h, :], ones2, W8[:, h * HALF:(h + 1) * HALF],
                                         start=True, stop=True).then_inc(s_pm, 1)
                return go

            tile(0)
            tile(1)
            for i in range(RT):
                n = 2 + 3 * i
                tile(n, bonus(i - 1) if i else None)
                pe.wait_ge(s_lo, 1)
                if i:
                    pe.wait_ge(s_bu, i)
                for h in range(2):
                    nc.tensor.matmul(ps[:, 6 + h, :], lora[0:LORA, i * P:(i + 1) * P],
                                     tdwa[0:LORA, h * HALF:(h + 1) * HALF], start=True, stop=True).then_inc(s_pm, 1)
                tile(n + 1)
                for h in range(2):
                    pe.wait_ge(s_sg, 4 * i + h + 1)
                    nc.tensor.matmul(ps[:, 6 + h, :], lora[LORA:P, i * P:(i + 1) * P],
                                     tdwa[LORA:P, h * HALF:(h + 1) * HALF], start=True, stop=True).then_inc(s_pm, 1)
                tile(n + 2)
                pe.wait_ge(s_sk, i + 1)
                for h in range(2):
                    pe.wait_ge(s_sg, 4 * i + 2 + h + 1)
                    nc.tensor.matmul(ps[:, 6 + h, :], ones2, W8[:, h * HALF:(h + 1) * HALF],
                                     start=True, stop=True).then_inc(s_pm, 1)
            with pe.Fori(0, RT) as i:
                for j in range(3):
                    pe.wait_ge(s_wcv[j], 16 * i + 16)
                    for h in range(2):
                        if j == 0:
                            pe.wait_ge(s_ccp, 2 * i + 1)
                            pe.wait_ge(s_pc, 2 * NR)
                        elif j == 1:
                            pe.wait_ge(s_u, 2 * i + 1)
                        else:
                            pe.wait_ge(s_cd, 2 * i + 1)
                        project((NR + j) % 3, ring_pair(NR + j), h).then_inc(s_pcv, 1)
            bonus(RT - 1)()

            heads = [(r, h) for r in range(RT) for h in range(2)]
            own = lambda h: slice(N * h, N * h + N)
            other = lambda h: slice(N * (1 - h), N * (1 - h) + N)
            pe.wait_ge(s_zv, 1)
            pe.wait_ge(s_bu, RT)
            with pe.Fori(0, NCH // 2) as it:
                for s in range(2):
                    b = 4 * s
                    pe.wait_ge(s_st[s], 48 * it + 48)
                    pe.wait_ge(s_yc[s], it + 1)
                    pe.wait_ge(s_s[s], it + 1)
                    for r, h in heads:
                        o = own(h)
                        last = nc.tensor.matmul(ps[:, b + h, r * P:(r + 1) * P],
                                                BKc[s][o, r, :, :].rearrange("p k t -> p (k t)"),
                                                ARc[s][o, r, :, :].rearrange("p k t -> p (k t)"), start=True, stop=True)
                    last.then_inc(s_g, 1)
                    for r, h in heads:
                        o = own(h)
                        last = nc.tensor.matmul(ps[other(h), b + 3, r * L:(r + 1) * L], Vc[s][o, r, :],
                                                cst[o, K_ID2:K_ID2 + L], start=True, stop=True)
                    last.then_inc(s_v, 1)
                    for r, h in heads:
                        o = own(h)
                        nc.tensor.matmul(ps[o, b + 2, r * L:(r + 1) * L], ARc[s][o, r, 0, :],
                                         BKc[s][o, r, h, :], start=True, stop=True)
                        last = nc.tensor.matmul(ps[o, b + 2, (RT + r) * L:(RT + r + 1) * L], ARc[s][o, r, 0, :],
                                                cst[o, K_ID2:K_ID2 + L], start=True, stop=True)
                    last.then_inc(s_m, 1)
                for s in range(2):
                    b = 4 * s
                    pe.wait_ge(s_bs, 2 * it + s + 1)
                    pe.wait_ge(s_ac, 2 * it + s + 1)
                    pe.sem_inc(s_pe_apart, 1)
                    for n, (r, h) in enumerate(heads):
                        o = own(h)
                        last = nc.tensor.transpose(ps[:, b + 3 - h, r * L:(r + 1) * L],
                                                   BKs[s][o, r, :, :].rearrange("p k t -> p (k t)"),
                                                   ident[o, N * h:N * h + N])
                    last.then_inc(s_bt, 1)
                for l in range(len(LEVELS)):
                    for s in range(2):
                        b = 4 * s
                        pe.wait_ge(s_t[s], 5 * it + l + 1)
                        if l == 0:
                            pe.wait_ge(s_mt, 2 * it + s + 1)
                            pe.wait_ge(s_gm[s], 2 * it + 2)
                        for r in range(RT):
                            last = nc.tensor.matmul(ps[:, b, r * L:(r + 1) * L], MTb[s][:, r].rearrange("p k t -> p (k t)"),
                                                    Tst[s][:, r, :], start=True, stop=True)
                        last.then_inc(s_pe_e[s], 1)
                    if l == 0:
                        for s in range(2):
                            b = 4 * s
                            pe.wait_ge(s_bc[s], 2 * it + 2)
                            pe.sem_inc(s_pe_apart, 1)
                            for n, (r, h) in enumerate(heads):
                                last = nc.tensor.matmul(ps[own(h), b + 3, r * L:(r + 1) * L], Gm[s][other(h), n, 0:L],
                                                        SAV[s][other(h), n, :], start=True, stop=True)
                            last.then_inc(s_nv, 1)
                    for s in range(2):
                        b = 4 * s
                        if l == 0:
                            pe.wait_ge(s_tt0[s], 2 * it + 2)
                        else:
                            pe.wait_ge(s_tt[s], 5 * it + l)
                        if l < 4:
                            pe.wait_ge(s_e[s], 10 * it + 2 * l + 1)
                            for r in range(RT):
                                last = nc.tensor.matmul(ps[:, b + 2, r * L:(r + 1) * L],
                                                        TTb[s][:, r].rearrange("p k t -> p (k t)"),
                                                        Est[s][:, r, :], start=True, stop=True)
                            last.then_inc(s_pe_f[s], 1)
                        pe.wait_ge(s_e[s], 10 * it + 2 * l + 2)
                        for r in range(RT):
                            last = nc.tensor.matmul(ps[:, b + 1, r * P:(r + 1) * P],
                                                    Ebd[s][:, r].rearrange("p k t -> p (k t)"),
                                                    TTb[s][:, r].rearrange("p k t -> p (k t)"), start=True, stop=True)
                        last.then_inc(s_pe_ft[s], 1)
                for s in range(2):
                    b = 4 * s
                    pe.wait_ge(s_tt[s], 5 * it + 5)
                    pe.wait_ge(s_nvc, 2 * it + s + 1)
                    pe.sem_inc(s_pe_apart, 1)
                    for r, h in heads:
                        last = nc.tensor.matmul(ps[own(h), b + 3, r * L:(r + 1) * L], MAt[s][own(h), 1, r, :],
                                                TTb[s][own(h), r, h, :], start=True, stop=True)
                    last.then_inc(s_ut, 1)
                for s in range(2):
                    b = 4 * s
                    pe.wait_ge(s_nvc, 2 * it + s + 1)
                    pe.wait_ge(s_utc, 2 * it + s + 1)
                    pe.wait_ge(s_bc[s], 2 * it + 2)
                    if s == 0:
                        pe.wait_ge(s_s[1], it + 1)
                    else:
                        pe.wait_ge(s_s[0], it + 2)
                    for r in range(RT):
                        nc.tensor.matmul(ps[:, b + 2, r * L:(r + 1) * L], TTb[s][:, r].rearrange("p k t -> p (k t)"),
                                         NVs[s][:, r, :], start=True, stop=False)
                        last = nc.tensor.matmul(ps[:, b + 2, r * L:(r + 1) * L],
                                                UTb[s][:, r].rearrange("p k t -> p (k t)"), St[s][:, r, :],
                                                start=False, stop=True)
                    last.then_inc(s_sa, 1)
                    pe.wait_ge(s_sac, 2 * it + s + 1)
                    for n, (r, h) in enumerate(heads):
                        last = nc.tensor.matmul(ps[own(h), b + 3, r * L:(r + 1) * L], BKt[s][:, n, :],
                                                SAV[s][:, n, :], start=True, stop=True)
                    last.then_inc(s_sn, 1)
                    for n, (r, h) in enumerate(heads):
                        nc.tensor.matmul(ps[own(h), b + 1, r * L:(r + 1) * L], SAV[s][:, n, :], Gm[s][:, n, L:2 * L],
                                         start=True, stop=False)
                        last = nc.tensor.matmul(ps[own(h), b + 1, r * L:(r + 1) * L], St[s][own(h), r, :],
                                                ARc[s][own(h), r, 1, :], start=False, stop=True)
                    last.then_inc(s_y[s], 1)

            for k in range(2):
                pe.wait_ge(s_yc[k], NCH // 2 + 1)
                pe.wait_ge(s_s[k], NCH // 2 + 1)
            pe.wait_ge(s_pi, 16 * (RT + 1))
            for i in range(RT):
                for h in range(2):
                    if i:
                        pe.wait_ge(s_yc2, 2 * i)
                    nc.tensor.matmul(ps[:, h, :], ones2, YF[:, i, h * HALF:(h + 1) * HALF],
                                     start=True, stop=True).then_inc(s_mp, 1)
                for h in range(2):
                    if i:
                        pe.wait_ge(s_mix, i)
                    nc.tensor.matmul(ps[:, 4 + h, :], wgate[:, i * P:(i + 1) * P], sdg[:, h * HALF:(h + 1) * HALF],
                                     start=True, stop=True).then_inc(s_gp, 1)
                pe.wait_ge(s_ysq, i + 1)
                for h in range(2):
                    nc.tensor.matmul(ps[:, 2 + h, :], ones2, gn_sq[i % 2][:, h * HALF:(h + 1) * HALF],
                                     start=True, stop=True).then_inc(s_vp, 1)

            pe.wait_ge(s_wo, 16 * (RT + 2))
            pe.wait_ge(s_mi, 3 * 16)
            pe.wait_ge(s_mix, RT)
            def out_project(t, h):
                if t >= 2:
                    pe.wait_ge(s_h, t - 1)
                for k in range(2 * RT):
                    last = nc.tensor.matmul(ps[:, 2 * (t % 2) + h, :], mixT[:, k, t * P:(t + 1) * P],
                                            wo[:, k, h * HALF:(h + 1) * HALF], start=k == 0, stop=k == 2 * RT - 1)
                last.then_inc(s_op, 1)

            for t in range(TT + 2):
                u = t - 1
                if t < TT:
                    out_project(t, 0)
                if 0 <= u < TT:
                    pe.wait_ge(s_xn2, u + 1)
                    for g in range(2):
                        if u:
                            pe.wait_ge(s_t2c, 2 * u + g - 1)
                        for k in range(4):
                            kt = 4 * g + k
                            last = nc.tensor.transpose(ps[:, 4 + g, k * P:(k + 1) * P], xn2[u % 2][:, kt * P:(kt + 1) * P],
                                                       ident)
                        last.then_inc(s_t2, 1)
                if t < TT:
                    out_project(t, 1)
                if 0 <= u < TT:
                    pe.wait_ge(s_t2c, 2 * u + 2)
                    if u:
                        pe.wait_ge(s_lgu, u)
                    for kt in range(KT):
                        last = nc.tensor.matmul(ps[:, 6, 0:E], xn2T[u % 2][:, kt, :], rw[:, kt, :],
                                                start=kt == 0, stop=kt == KT - 1)
                    last.then_inc(s_lg, 1)
                if t >= 2:
                    u = t - 2
                    pe.wait_ge(s_hot, u + 1)
                    if u:
                        pe.wait_ge(s_rku, u)
                    nc.tensor.matmul(ps[:, 7, 0:E], tri, hots[u % 2], start=True, stop=True)
                    nc.tensor.matmul(ps[:, 7, E:2 * E], ones, hots[u % 2], start=True, stop=True).then_inc(s_rank, 1)
            pe.wait_ge(s_rku, TT)

            def transpose_tokens(m, q):
                for k in range(2):
                    kt = 2 * q + k
                    nc.tensor.transpose(ps[:, 4 + q % 2, k * C:k * C + P], xg[:, kt * P:(kt + 1) * P], ident)
                    last = nc.tensor.transpose(ps[:, 4 + q % 2, k * C + P:(k + 1) * C],
                                               xg2[:, kt * P:(kt + 1) * P], ident)
                last.then_inc(s_xt, 1)

            def transpose_rows(half, size):
                for k in range(4):
                    last = nc.tensor.transpose(ps[:, 6 + half, k * P:(k + 1) * P], yT[:, 4 * half + k, 0:P], ident)
                if size > P:
                    last.then_inc(s_yt, 1)
                    for k in range(4):
                        last = nc.tensor.transpose(ps[:, half, k * P:(k + 1) * P], yT[:, 4 * half + k, P:C], ident)
                    last.then_inc(s_yt, 1)
                else:
                    last.then_inc(s_yt, 2)

            def expert_products(n, m, size):
                for f in range(KT):
                    u = f // 2
                    if f % 2 == 0:
                        pe.wait_ge(s_wt[u], 16 * n + 16)
                    if f < 2:
                        pe.wait_ge(s_ye, 4 * n + 1 + 2 * f)
                    else:
                        pe.wait_ge(s_gd, 8 * n + f - 1)
                    for k in range(2):
                        for kt in range(KT):
                            if f == 0 and k == 0 and kt in (0, 4, 6):
                                pe.wait_ge(s_xe, 4 * m - {0: 2, 4: 1, 6: 0}[kt])
                            o = f % 2 * 2 * P + k
                            last = nc.tensor.matmul(ps[:, f % 2, k * C:k * C + size],
                                                    wslot[u][:, kt, o:o + 2 * P - 1:2], xT[:, kt, 0:size],
                                                    start=kt == 0, stop=kt == KT - 1)
                    last.then_inc(s_gu, 1)
                pe.wait_ge(s_gx, 32 * m + 32)
                transpose_tokens(m, 0)
                transpose_tokens(m, 1)
                for d in range(KT):
                    u = 4 + d // 4
                    if d % 4 == 0:
                        pe.wait_ge(s_wt[u], 16 * n + 16)
                    if d >= 2:
                        pe.wait_ge(s_dd, 8 * n + d - 1)
                    for ft in range(KT):
                        if d == 0 and ft in (0, KT - 1):
                            pe.wait_ge(s_act, 8 * n + (KT if ft else KT - 1))
                        last = nc.tensor.matmul(ps[:, 2 + d % 2, 0:size], wslot[u][:, ft, d % 4 * P:(d % 4 + 1) * P],
                                                actT[:, ft, 0:size], start=ft == 0, stop=ft == KT - 1)
                    last.then_inc(s_dn, 1)
                    if d == KT - 3:
                        pe.wait_ge(s_ye, 4 * n + 3)
                        transpose_rows(0, size)
                pe.wait_ge(s_xe, 4 * m + 2)
                transpose_tokens(m, 2)
                transpose_tokens(m, 3)
                pe.wait_ge(s_dd, 8 * n + 8)
                transpose_rows(1, size)

            def by_size(need, lo, hi, n, m):
                if lo == hi:
                    expert_products(n, m, SIZES[lo])
                    return
                mid = (lo + hi) // 2
                with pe.If(need > mid):
                    by_size(need, mid + 1, hi, n, m)
                with pe.Else():
                    by_size(need, lo, mid, n, m)

            def expert_pe(r):
                pe.wait_ge(s_sz, 1)
                m = r * (E + 1)
                pe.wait_ge(s_gx, 32 * m + 32)
                for q in range(4):
                    if q >= 2:
                        pe.wait_ge(s_xe, 4 * m + q - 1)
                    transpose_tokens(m, q)
                with pe.Fori(0, E) as e:
                    n = r * E + e
                    need = pe.value_load(size_i[0:1, bass.ds(n, 1)], min_val=0, max_val=len(SIZES) - 1)
                    by_size(need, 0, len(SIZES) - 1, n, r * (E + 1) + e + 1)
                pe.wait_ge(s_xe, 4 * (r + 1) * (E + 1))

            rounds(pe, expert_pe)

            pe.wait_ge(s_md, 1)
            for t in range(TT):
                last = nc.tensor.transpose(ps[0:E, t // 4, t % 4 * P:(t % 4 + 1) * P], G[:, t, :], ident)
            last.then_inc(s_bp, 1)
            pe.wait_ge(s_gTc, 1)
            pe.wait_ge(s_fi, 32)
            pe.wait_ge(s_fs, 1)
            for t in range(TT):
                if t >= 2:
                    pe.wait_ge(s_hf, t - 1)
                for h in range(2):
                    bank, w = ps[:, 2 + 2 * (t % 2) + h, :], slice(h * HALF, (h + 1) * HALF)
                    nc.tensor.matmul(bank, GT[0:E, t, :], dnb[0:E, w], start=True, stop=False)
                    if h == 0:
                        pe.wait_ge(s_yl[t % 3], 16 * (t // 3 + 1))
                    nc.tensor.matmul(bank, dgate[:, t, :], ypair[t % 3][:, 0, w], start=False, stop=True
                                     ).then_inc(s_bp, 1)


IN_TILES = ([3072, 3200] + [1536 + k * 512 + i * P for i in range(4) for k in range(3)]
            + [[512, 1024, 0][k] + i * P for i in range(4) for k in range(3)])


def kernel(**a):
    import concourse.bacc as _bacc
    from concourse.bass_utils import run_bass_kernel_spmd as _run

    a = {k: np.asarray(v) for k, v in a.items()}
    nc = _bacc.Bacc("TRN2", target_bir_lowering=False, num_devices=1)

    def cols(v):
        return v.reshape(-1, P).T

    conv = a["conv_w"][0].reshape(3, RT, P).transpose(2, 1, 0).reshape(P, 12)
    prm = np.ascontiguousarray(np.concatenate(
        [cols(a["mu_shift"][0]), cols(a["w0"][0]), cols(a["a0"][0]), cols(a["k_k"][0]), cols(a["k_a"][0]),
         cols(a["r_k"][0].reshape(-1)), cols(a["ln_x_w"][0]), cols(a["ln_x_b"][0]), conv], axis=1))
    w_in = a["w_in"][0]
    w_in_t = np.stack([w_in[:, o:o + P].reshape(KT, P, P).transpose(1, 0, 2).reshape(P, KT * P) for o in IN_TILES])
    rep = lambda v: np.ascontiguousarray(np.broadcast_to(v, (P, v.shape[-1])))
    arrays = {
        "x": a["x"][0],
        "w_in_t": w_in_t,
        "prm": prm,
        "lora": np.concatenate([a["w_decay_up"][0], a["w_iclr_up"][0]]),
        "wgate": a["w_gate_up"][0],
        "normw": np.stack([rep(a["norm_mix_w"][0]), rep(a["norm_ffn_w"][0]), rep(a["norm_final_w"])]),
        "w_out": a["w_out"][0],
        "router_w": a["router_w"][0],
        "router_b": rep(a["router_b"][0]),
        "gub": np.ascontiguousarray(a["gu_b"][0].reshape(E, KT, P, 2).transpose(2, 0, 1, 3).reshape(P, E * 2 * KT)),
        "gu_w": a["gu_w"][0],
        "dn_w": a["dn_w"][0],
        "dn_b": a["dn_b"][0],
        "consts": constants(),
        "list0": np.tile(np.array([[SKIP, SKIP]], np.int32), ((E + 1) * LIST, 1)),
    }
    arrays = {k: np.ascontiguousarray(v) for k, v in arrays.items()}
    args = [nc.dram_tensor(n, v.shape, mybir.dt.from_np(v.dtype), kind="ExternalInput").ap()
            for n, v in arrays.items()]
    out = nc.dram_tensor("out", (T, D), FP, kind="ExternalOutput").ap()
    scratch = [("conv_s", (RT, P, T), FP), ("bonus_s", (RT, P, T), FP), ("xn_s", (T, D), FP),
               ("pair_s", (PAIRS, D), FP), ("list_s", ((E + 1) * LIST, 2), I32), ("flag_s", (1, 8), I32)]
    args.append(out)
    args += [nc.dram_tensor(n, s, d, kind="Internal").ap() for n, s, d in scratch]
    build(nc, *args)
    r = _run(nc, [arrays], core_ids=[0])
    return r.results[0]["out"].reshape(1, T, D)
```
